# Optimizing a Trainium2 kernel written in Bass

```python
import math
import functools
import jax
import jax.numpy as jnp
from jax import lax
import numpy as np

D_MODEL = 2048
BATCH = 1
SEQ = 256
DEPTH = 1
DEC_BATCH = 8
DEC_SEQ = 4
PAST_LEN = 256
PAGE_SIZE = 128

N_HEADS = 16
N_KV_HEADS = 4
GROUP = N_HEADS // N_KV_HEADS
HEAD_DIM = 64
CMP_STRIDE = 16
CMP_LEN = 2 * CMP_STRIDE
SEL_LEN = 64
N_SEL = 16
WINDOW = 512
Q_BLOCK = 128
FORCE_BONUS = 1e3
N_BUCKETS = 32
MAX_DISTANCE = 128
D_RNN = 1024
N_RNN_BLOCKS = 16
RNN_BLOCK = D_RNN // N_RNN_BLOCKS
CONV_WIDTH = 4
LRU_C = 8.0
D_FF = ((8 * D_MODEL + 3 * 256 - 1) // (3 * 256)) * 256
ALPHA = (2.0 * DEPTH) ** 0.25
BETA = (8.0 * DEPTH) ** -0.25
Q_W = N_HEADS * HEAD_DIM
KV_W = 2 * N_KV_HEADS * HEAD_DIM
IN_SPLITS = (Q_W, KV_W, KV_W, KV_W, 3 * N_HEADS, D_RNN, D_RNN, 2 * D_MODEL)
N_IN = Q_W + 3 * KV_W + 3 * N_HEADS + 2 * D_RNN + 2 * D_MODEL

kernel_name = 'nsa_rglru_hybrid_step'

def layer_norm(x, g, b, eps=1e-5):
    xf = x.astype(jnp.float32)
    mu = xf.mean(-1, keepdims=True)
    var = jnp.square(xf - mu).mean(-1, keepdims=True)
    return ((xf - mu) * lax.rsqrt(var + eps)).astype(x.dtype) * g + b

def masked_softmax(s, mask):
    s = jnp.where(mask, s.astype(jnp.float32), -1e30)
    p = jnp.exp(s - jnp.max(s, -1, keepdims=True)) * mask
    return p / jnp.maximum(p.sum(-1, keepdims=True), 1e-30)

def t5_bucket(dist):
    n = jnp.maximum(dist, 0)
    exact = N_BUCKETS // 2
    log_ratio = jnp.log(jnp.maximum(n, 1).astype(jnp.float32) / exact) / math.log(MAX_DISTANCE / exact)
    large = jnp.minimum(exact + (log_ratio * (N_BUCKETS - exact)).astype(jnp.int32), N_BUCKETS - 1)
    return jnp.where(n < exact, n, large)

def cmp_to_sel(n_cmp, n_sel):
    j = np.arange(n_cmp)[:, None]
    s = np.arange(n_sel)[None, :]
    lo = np.maximum(j * CMP_STRIDE, s * SEL_LEN)
    hi = np.minimum(j * CMP_STRIDE + CMP_LEN, (s + 1) * SEL_LEN)
    return jnp.asarray(np.maximum(hi - lo, 0) / CMP_LEN, dtype=jnp.float32)

def compress(rows, pos_emb, w1, w2):
    B, T = rows.shape[0], rows.shape[1]
    r = rows.reshape(B, T // CMP_STRIDE, CMP_STRIDE, N_KV_HEADS, HEAD_DIM)
    w1h = w1.reshape(2, CMP_STRIDE, HEAD_DIM, HEAD_DIM)
    pe = pos_emb.reshape(2, CMP_STRIDE, 1, HEAD_DIM)
    lead = jnp.einsum('bnlgd,lde->bnge', r + pe[0], w1h[0])
    tail = jnp.einsum('bnlgd,lde->bnge', r + pe[1], w1h[1])
    return jnp.einsum('bnge,ef->bngf', jax.nn.silu(lead[:, :-1] + tail[:, 1:]), w2)

def nsa_attend(q, qpos, gates, kc, vc, k_sel, v_sel, kw, vw, kwpos, rel_bias):
    B, Q = q.shape[0], q.shape[1]
    n_cmp, n_sel = kc.shape[1], k_sel.shape[1]
    scale = HEAD_DIM ** -0.5
    tbl = rel_bias.reshape(N_BUCKETS, N_KV_HEADS, GROUP)
    c_end = jnp.arange(n_cmp) * CMP_STRIDE + (CMP_LEN - 1)
    dist_c = qpos[:, None] - c_end[None, :]
    bias_c = tbl[t5_bucket(dist_c)].transpose(0, 2, 3, 1)
    s_c = jnp.einsum('bqgrd,bngd->bqgrn', q, kc) * scale + bias_c[None]
    p_c = masked_softmax(s_c, (dist_c >= 0)[None, :, None, None, :])
    o_c = jnp.einsum('bqgrn,bngd->bqgrd', p_c.astype(vc.dtype), vc)
    imp = jnp.einsum('bqgn,ns->bqgs', p_c.sum(3), cmp_to_sel(n_cmp, n_sel))
    blk = jnp.arange(n_sel)[None, :]
    cur = (qpos // SEL_LEN)[:, None]
    forced = (blk == 0) | (blk == cur) | (blk == cur - 1)
    imp = jnp.where(forced[None, :, None, :], imp + FORCE_BONUS, imp)
    imp = jnp.where((blk <= cur)[None, :, None, :], imp, -1e30)
    top_val, top_idx = lax.top_k(imp, min(N_SEL, n_sel))
    top_ok = top_val > -1e29
    b_i = jnp.arange(B)[:, None, None, None]
    g_i = jnp.arange(N_KV_HEADS)[None, None, :, None]
    k_s = k_sel.transpose(0, 3, 1, 2, 4)[b_i, g_i, top_idx]
    v_s = v_sel.transpose(0, 3, 1, 2, 4)[b_i, g_i, top_idx]
    pos_s = top_idx[..., None] * SEL_LEN + jnp.arange(SEL_LEN)
    dist_s = qpos[None, :, None, None, None] - pos_s
    mask_s = (dist_s >= 0) & top_ok[..., None]
    bias_s = tbl[t5_bucket(dist_s), g_i[..., None]]
    s_s = jnp.einsum('bqgrd,bqgnld->bqgrnl', q, k_s) * scale + bias_s.transpose(0, 1, 2, 5, 3, 4)
    n_keys = s_s.shape[-2] * SEL_LEN
    p_s = masked_softmax(s_s.reshape(B, Q, N_KV_HEADS, GROUP, n_keys), mask_s.reshape(B, Q, N_KV_HEADS, 1, n_keys))
    o_s = jnp.einsum('bqgrm,bqgmd->bqgrd', p_s.astype(v_s.dtype), v_s.reshape(B, Q, N_KV_HEADS, n_keys, HEAD_DIM))
    dist_w = qpos[:, None] - kwpos[None, :]
    mask_w = (dist_w >= 0) & (dist_w < WINDOW) & (kwpos >= 0)[None, :]
    bias_w = tbl[t5_bucket(dist_w)].transpose(0, 2, 3, 1)
    s_w = jnp.einsum('bqgrd,bkgd->bqgrk', q, kw) * scale + bias_w[None]
    p_w = masked_softmax(s_w, mask_w[None, :, None, None, :])
    o_w = jnp.einsum('bqgrk,bkgd->bqgrd', p_w.astype(vw.dtype), vw)
    o = gates[..., 0:1] * o_c + gates[..., 1:2] * o_s + gates[..., 2:3] * o_w
    return o.reshape(B, Q, N_HEADS * HEAD_DIM)

def nsa_prompt(q, kvc, kvs, kvw, gates, cmp_pos, cmp_w1, cmp_w2, rel_bias):
    B, T = q.shape[0], q.shape[1]
    kc = compress(kvc[:, :, 0], cmp_pos[0], cmp_w1[0], cmp_w2[0])
    vc = compress(kvc[:, :, 1], cmp_pos[1], cmp_w1[1], cmp_w2[1])
    blocks = kvs.reshape(B, T // SEL_LEN, SEL_LEN, 2, N_KV_HEADS, HEAD_DIM)
    kw_pad = jnp.pad(kvw, ((0, 0), (WINDOW, 0), (0, 0), (0, 0), (0, 0)))

    def one_block(i):
        q0 = i * Q_BLOCK
        qb = lax.dynamic_slice_in_dim(q, q0, Q_BLOCK, axis=1)
        gb = lax.dynamic_slice_in_dim(gates, q0, Q_BLOCK, axis=1)
        wb = lax.dynamic_slice_in_dim(kw_pad, q0, WINDOW + Q_BLOCK, axis=1)
        qpos = q0 + jnp.arange(Q_BLOCK)
        kwpos = q0 - WINDOW + jnp.arange(WINDOW + Q_BLOCK)
        return nsa_attend(qb, qpos, gb, kc, vc, blocks[:, :, :, 0], blocks[:, :, :, 1],
                          wb[:, :, 0], wb[:, :, 1], kwpos, rel_bias)

    out = lax.map(one_block, jnp.arange(T // Q_BLOCK))
    return out.transpose(1, 0, 2, 3).reshape(B, T, N_HEADS * HEAD_DIM)

def nsa_sample(q, kvc, kvs, kvw, gates, cache_c, cache_s, win_buf, page_table, cmp_pos, cmp_w1, cmp_w2, rel_bias):
    B, S = q.shape[0], q.shape[1]
    past = page_table.shape[1] * PAGE_SIZE

    def full_rows(cache, new, mult):
        rows = jnp.concatenate([cache[page_table].reshape(B, past, 2, N_KV_HEADS, HEAD_DIM), new.astype(cache.dtype)], axis=1)
        pad = -(past + S) % mult
        return jnp.pad(rows, ((0, 0), (0, pad), (0, 0), (0, 0), (0, 0)))

    rows_c = full_rows(cache_c, kvc, CMP_STRIDE)
    kc = compress(rows_c[:, :, 0], cmp_pos[0], cmp_w1[0], cmp_w2[0])
    vc = compress(rows_c[:, :, 1], cmp_pos[1], cmp_w1[1], cmp_w2[1])
    rows_s = full_rows(cache_s, kvs, SEL_LEN)
    blocks = rows_s.reshape(B, -1, SEL_LEN, 2, N_KV_HEADS, HEAD_DIM)
    n_buf = win_buf.shape[1]
    rows_w = jnp.concatenate([win_buf, kvw.astype(win_buf.dtype)], axis=1)
    qpos = past + jnp.arange(S)
    kwpos = past - n_buf + jnp.arange(n_buf + S)
    return nsa_attend(q, qpos, gates, kc, vc, blocks[:, :, :, 0], blocks[:, :, :, 1],
                      rows_w[:, :, 0], rows_w[:, :, 1], kwpos, rel_bias)

def causal_conv(x, buf, w, b):
    T = x.shape[1]
    xp = jnp.concatenate([buf.astype(x.dtype), x], axis=1)
    y = xp[:, CONV_WIDTH - 1:] * w[CONV_WIDTH - 1] + b
    for k in range(CONV_WIDTH - 1):
        y = y + xp[:, k:k + T] * w[k]
    return y, xp[:, T:]

def rg_lru(x, h0, w_a, b_a, w_i, b_i, lam):
    B, T = x.shape[0], x.shape[1]
    xb = x.reshape(B, T, N_RNN_BLOCKS, RNN_BLOCK)
    r = jax.nn.sigmoid(jnp.einsum('btnd,nde->btne', xb, w_a).reshape(B, T, D_RNN) + b_a)
    i = jax.nn.sigmoid(jnp.einsum('btnd,nde->btne', xb, w_i).reshape(B, T, D_RNN) + b_i)
    log_a = -LRU_C * r.astype(jnp.float32) * jax.nn.softplus(-lam.astype(jnp.float32))
    u = jnp.sqrt(-jnp.expm1(2.0 * log_a)) * (i * x).astype(jnp.float32)

    def step(h, inp):
        a_t, u_t = inp
        h = a_t * h + u_t
        return h, h

    h_last, hs = lax.scan(step, h0.astype(jnp.float32), (jnp.exp(log_a).swapaxes(0, 1), u.swapaxes(0, 1)))
    return hs.swapaxes(0, 1).astype(x.dtype), h_last.astype(x.dtype)

def mixer(h, attend, conv_buf, h0, lp):
    B, T = h.shape[0], h.shape[1]
    proj = h @ lp['w_in'] + lp['b_in']
    cuts = [int(v) for v in np.cumsum(IN_SPLITS)[:-1]]
    q, kvc, kvs, kvw, nsa_g, r_x, r_y, merge_g = jnp.split(proj, cuts, axis=-1)
    kv_shape = (B, T, 2, N_KV_HEADS, HEAD_DIM)
    kvc = kvc.reshape(kv_shape)
    kvs = kvs.reshape(kv_shape)
    kvw = kvw.reshape(kv_shape)
    gates = jax.nn.sigmoid(nsa_g).reshape(B, T, N_KV_HEADS, GROUP, 3)
    o_attn = attend(q.reshape(B, T, N_KV_HEADS, GROUP, HEAD_DIM), kvc, kvs, kvw, gates) @ lp['w_attn_o']
    xc, conv_new = causal_conv(r_x, conv_buf, lp['conv_w'], lp['conv_b'])
    hs, h_last = rg_lru(xc, h0, lp['lru_wa'], lp['lru_ba'], lp['lru_wi'], lp['lru_bi'], lp['lru_lambda'])
    o_rnn = (hs * jax.nn.gelu(r_y)) @ lp['w_rnn_o']
    g_attn, g_rnn = jnp.split(jax.nn.sigmoid(merge_g), 2, axis=-1)
    out = (g_attn * o_attn + g_rnn * o_rnn) @ lp['w_out']
    return out, (kvc, kvs, kvw, conv_new, h_last)

def trunk_layer(x, c, attend, conv_buf, h0, lp):
    ada = jax.nn.silu(c) @ lp['w_ada'] + lp['b_ada']
    sh1, sc1, g1, sh2, sc2, g2 = [a[:, None, :] for a in jnp.split(ada, 6, axis=-1)]
    mix, states = mixer(x * (1 + sc1) + sh1, attend, conv_buf, h0, lp)
    x = layer_norm(ALPHA * x + (1 + g1) * mix, lp['ln_g'][0], lp['ln_b'][0])
    gt, up = jnp.split((x * (1 + sc2) + sh2) @ lp['w_ffn_in'], 2, axis=-1)
    f = (jax.nn.silu(gt) * up) @ lp['w_ffn_out']
    x = layer_norm(ALPHA * x + (1 + g2) * f, lp['ln_g'][1], lp['ln_b'][1])
    return x, states

def setup_inputs(seed: int = 0) -> dict:
    key = jax.random.key(seed)
    ks = jax.random.split(key, 32)
    f32 = jnp.float32

    def nrm(k, shape, scale):
        return jax.random.normal(k, shape, f32) * scale

    n_pages = PAST_LEN // PAGE_SIZE
    n_used = DEC_BATCH * n_pages
    n_phys = n_used + max(1, n_used // 4)
    win_rows = min(WINDOW, PAST_LEN)
    kv_paged = (DEPTH, n_phys, PAGE_SIZE, 2, N_KV_HEADS, HEAD_DIM)
    page_table = jax.random.permutation(ks[9], n_phys)[:n_used].reshape(DEC_BATCH, n_pages).astype(jnp.int32)
    u = jax.random.uniform(ks[25], (DEPTH, D_RNN), f32, 0.9, 0.999)
    a_base = u ** (1.0 / LRU_C)
    lru_lambda = jnp.log(a_base) - jnp.log1p(-a_base)
    return {
        'x_prompt': nrm(ks[0], (BATCH, SEQ, D_MODEL), 1.0),
        'x_sample': nrm(ks[1], (DEC_BATCH, DEC_SEQ, D_MODEL), 1.0),
        'c_prompt': nrm(ks[2], (BATCH, D_MODEL), 1.0),
        'c_sample': nrm(ks[3], (DEC_BATCH, D_MODEL), 1.0),
        'cache_cmp_kv': nrm(ks[4], kv_paged, 1.0),
        'cache_slc_kv': nrm(ks[5], kv_paged, 1.0),
        'cache_win_kv': nrm(ks[6], (DEPTH, DEC_BATCH, win_rows, 2, N_KV_HEADS, HEAD_DIM), 1.0),
        'state_conv': nrm(ks[7], (DEPTH, DEC_BATCH, CONV_WIDTH - 1, D_RNN), 1.0),
        'state_rnn_h': nrm(ks[8], (DEPTH, DEC_BATCH, D_RNN), 0.5),
        'page_table': page_table,
        'rel_bias': nrm(ks[10], (N_BUCKETS, N_HEADS), 0.5),
        'w_ada': nrm(ks[11], (DEPTH, D_MODEL, 6 * D_MODEL), 0.2 * D_MODEL ** -0.5),
        'b_ada': nrm(ks[12], (DEPTH, 6 * D_MODEL), 0.01),
        'w_in': nrm(ks[13], (DEPTH, D_MODEL, N_IN), D_MODEL ** -0.5),
        'b_in': nrm(ks[14], (DEPTH, N_IN), 0.01),
        'cmp_pos': nrm(ks[15], (DEPTH, 2, CMP_LEN, HEAD_DIM), 0.1),
        'cmp_w1': nrm(ks[16], (DEPTH, 2, CMP_LEN, HEAD_DIM, HEAD_DIM), (CMP_LEN * HEAD_DIM) ** -0.5),
        'cmp_w2': nrm(ks[17], (DEPTH, 2, HEAD_DIM, HEAD_DIM), HEAD_DIM ** -0.5),
        'w_attn_o': nrm(ks[18], (DEPTH, Q_W, D_MODEL), Q_W ** -0.5),
        'conv_w': nrm(ks[19], (DEPTH, CONV_WIDTH, D_RNN), CONV_WIDTH ** -0.5),
        'conv_b': nrm(ks[20], (DEPTH, D_RNN), 0.01),
        'lru_wa': nrm(ks[21], (DEPTH, N_RNN_BLOCKS, RNN_BLOCK, RNN_BLOCK), RNN_BLOCK ** -0.5),
        'lru_ba': nrm(ks[22], (DEPTH, D_RNN), 0.01),
        'lru_wi': nrm(ks[23], (DEPTH, N_RNN_BLOCKS, RNN_BLOCK, RNN_BLOCK), RNN_BLOCK ** -0.5),
        'lru_bi': nrm(ks[24], (DEPTH, D_RNN), 0.01),
        'lru_lambda': lru_lambda,
        'w_rnn_o': nrm(ks[26], (DEPTH, D_RNN, D_MODEL), D_RNN ** -0.5),
        'w_out': nrm(ks[27], (DEPTH, D_MODEL, D_MODEL), BETA * D_MODEL ** -0.5),
        'w_ffn_in': nrm(ks[28], (DEPTH, D_MODEL, 2 * D_FF), D_MODEL ** -0.5),
        'w_ffn_out': nrm(ks[29], (DEPTH, D_FF, D_MODEL), BETA * D_FF ** -0.5),
        'ln_g': 1.0 + nrm(ks[30], (DEPTH, 2, D_MODEL), 0.01),
        'ln_b': nrm(ks[31], (DEPTH, 2, D_MODEL), 0.01),
    }

def reference(x_prompt, x_sample, c_prompt, c_sample, cache_cmp_kv, cache_slc_kv, cache_win_kv, state_conv,
              state_rnn_h, page_table, rel_bias, w_ada, b_ada, w_in, b_in, cmp_pos, cmp_w1, cmp_w2, w_attn_o,
              conv_w, conv_b, lru_wa, lru_ba, lru_wi, lru_bi, lru_lambda, w_rnn_o, w_out, w_ffn_in, w_ffn_out,
              ln_g, ln_b):
    y_p, y_s = x_prompt, x_sample
    st_p, st_s = [], []
    n_keep = min(WINDOW, x_prompt.shape[1])
    for l in range(DEPTH):
        lp = {'w_ada': w_ada[l], 'b_ada': b_ada[l], 'w_in': w_in[l], 'b_in': b_in[l], 'w_attn_o': w_attn_o[l],
              'conv_w': conv_w[l], 'conv_b': conv_b[l], 'lru_wa': lru_wa[l], 'lru_ba': lru_ba[l],
              'lru_wi': lru_wi[l], 'lru_bi': lru_bi[l], 'lru_lambda': lru_lambda[l], 'w_rnn_o': w_rnn_o[l],
              'w_out': w_out[l], 'w_ffn_in': w_ffn_in[l], 'w_ffn_out': w_ffn_out[l], 'ln_g': ln_g[l],
              'ln_b': ln_b[l]}
        attend_p = functools.partial(nsa_prompt, cmp_pos=cmp_pos[l], cmp_w1=cmp_w1[l], cmp_w2=cmp_w2[l],
                                     rel_bias=rel_bias)
        attend_s = functools.partial(nsa_sample, cache_c=cache_cmp_kv[l], cache_s=cache_slc_kv[l],
                                     win_buf=cache_win_kv[l], page_table=page_table, cmp_pos=cmp_pos[l],
                                     cmp_w1=cmp_w1[l], cmp_w2=cmp_w2[l], rel_bias=rel_bias)
        zero_buf = jnp.zeros((x_prompt.shape[0], CONV_WIDTH - 1, D_RNN), x_prompt.dtype)
        zero_h = jnp.zeros((x_prompt.shape[0], D_RNN), jnp.float32)
        y_p, (kc, ksl, kw, cv, hh) = trunk_layer(y_p, c_prompt, attend_p, zero_buf, zero_h, lp)
        st_p.append((kc, ksl, kw[:, kw.shape[1] - n_keep:], cv, hh))
        y_s, sts = trunk_layer(y_s, c_sample, attend_s, state_conv[l], state_rnn_h[l], lp)
        st_s.append(sts)
    new_cmp_kv_prompt = jnp.stack([s[0] for s in st_p])
    new_slc_kv_prompt = jnp.stack([s[1] for s in st_p])
    new_win_kv_prompt = jnp.stack([s[2] for s in st_p])
    new_conv_prompt = jnp.stack([s[3] for s in st_p])
    new_rnn_h_prompt = jnp.stack([s[4] for s in st_p])
    new_cmp_kv_sample = jnp.stack([s[0] for s in st_s])
    new_slc_kv_sample = jnp.stack([s[1] for s in st_s])
    new_win_kv_sample = jnp.stack([s[2] for s in st_s])
    new_conv_sample = jnp.stack([s[3] for s in st_s])
    new_rnn_h_sample = jnp.stack([s[4] for s in st_s])
    return (y_p, y_s, new_cmp_kv_prompt, new_slc_kv_prompt, new_win_kv_prompt, new_conv_prompt, new_rnn_h_prompt,
            new_cmp_kv_sample, new_slc_kv_sample, new_win_kv_sample, new_conv_sample, new_rnn_h_sample)


_drawn_inputs = setup_inputs


def setup_inputs(seed=0):
    import zlib

    import numpy as np

    out = dict(_drawn_inputs(seed))
    spreads = {}
    factors = {'cache_slc_kv': 3.245,
     'cache_win_kv': 3.312,
     'cmp_pos': 6.957,
     'lru_ba': 26.643,
     'lru_bi': 8.0,
     'ln_g': 12.711,
     'ln_b': 13.2}
    for name, (base, spread) in spreads.items():
        noise = np.random.default_rng([zlib.crc32(name.encode()), seed]).standard_normal(out[name].shape)
        drawn = base * np.exp(spread * noise) if base else spread * noise
        out[name] = jnp.asarray(drawn.astype(out[name].dtype))
    for name, factor in factors.items():
        out[name] = (out[name] * factor).astype(out[name].dtype)
    return out
```

```python
from contextlib import ExitStack

import concourse.bass as bass
from concourse import mybir

F32 = mybir.dt.float32
F32R = mybir.dt.float32r
I32 = mybir.dt.int32
ACT = mybir.ActivationFunctionType
ALU = mybir.AluOpType
AX = mybir.AxisListType

P = 128
D = 2048
DC = D // P
TP, DEC_B, DEC_S = 256, 8, 4
TS = DEC_B * DEC_S
T = TP + TS
NSEQ = 1 + DEC_B
H, KVH, HD = 16, 4, 64
NP_ = 8
PAST, PAGE = 256, 128
STRIDE, CMP = 16, 32
NCMP = PAST // STRIDE - 1
DR = 1024
RC = DR // P
FF = 5632
FC = FF // P
HALF = FC // 2
KS = HALF // 2
ALPHA = 2.0 ** 0.25
LRU_C = 8.0
SCALE = HD ** -0.5
EPS = 1e-5
NEG = -1e30
UNIT = DC * P
KUNIT = KS * P
RAW_SLOTS = 4
LPAD = 3 + TP + 7 * DEC_B
L = LPAD - 3
S0 = TP + 3
RV = 384
NADA = 6 * DC


class Stage:

    def __init__(self, pattern, n, r0, g0, a0=0):
        self.n, self.r0, self.g0, self.a0, self.U = n, r0, g0, a0, len(pattern)
        self.G = [p for p, c in enumerate(pattern) if c == "G"]
        self.A = [p for p, c in enumerate(pattern) if c == "A"]
        assert r0 % RAW_SLOTS == 0 and self.U % RAW_SLOTS == 0 and len(self.G) % 2 == 0
        self.r_end, self.g_end, self.a_end = r0 + n * self.U, g0 + n * len(self.G), a0 + n * len(self.A)

    def raw(self, i, pos):
        return pos % RAW_SLOTS, i * (self.U // RAW_SLOTS) + (self.r0 + pos) // RAW_SLOTS

    def rawG(self, i, j):
        return self.raw(i, self.G[j] if j < len(self.G) else self.U)

    def g(self, i, j):
        return i * len(self.G) + (self.g0 + j)


INIT = Stage("AAAA", 8, 0, 0, 0)
QS = Stage("GGGG", 2, INIT.r_end, 1)
KVS = Stage("GGGG", 3, QS.r_end, QS.g_end)
RNN = Stage("GAAGAAGAAGAA", 4, KVS.r_end, KVS.g_end, INIT.a_end)
MRG = Stage("GGGG", 8, RNN.r_end, RNN.g_end)
CMB = Stage("GAAGGAAG", 4, MRG.r_end, MRG.g_end, RNN.a_end)
OUT = Stage("GAAGGAAG", 4, CMB.r_end, CMB.g_end, CMB.a_end)
FIN = [None, None]
FOUT = [None, None]
FIN[0] = Stage("GGGG", 11, OUT.r_end, OUT.g_end)
FOUT[0] = Stage("GGGG", 8, FIN[0].r_end, FIN[0].g_end)
FIN[1] = Stage("GGGG", 11, FOUT[0].r_end, FOUT[0].g_end)
FOUT[1] = Stage("GGGG", 8, FIN[1].r_end, FIN[1].g_end)
assert OUT.a_end == NADA
O_FIN = [FIN[0].g0, FIN[0].g_end + 16]
O_FOUT = [FIN[0].g_end, FIN[0].g_end + 16 + 2 * HALF]


class Chain:

    def __init__(self, eng, sem):
        self.eng, self.sem, self.n, self.i, self.per = eng, sem, 0, None, 0

    def loop(self, i, per):
        self.i, self.per, self.k = i, per, 0

    def end(self, times):
        assert self.k == self.per, f"{self.k} steps, {self.per} said"
        self.n, self.i = self.n + self.per * times, None

    def mark(self, ins):
        ins.then_inc(self.sem, 1)
        if self.i is None:
            self.n += 1
            return self.n
        self.k += 1
        return self.i * self.per + (self.n + self.k)

    def wait(self, value):
        self.eng.wait_ge(self.sem, value)

    def __call__(self, ins):
        self.wait(self.mark(ins))


def build(nc, a, out):
    with ExitStack() as ctx:
        def sem(name):
            return ctx.enter_context(nc.semaphore(name))

        def sbuf(stack, name, shape, dt=F32):
            return stack.enter_context(nc.sbuf_tensor(name, shape, dt))

        def dram(name, shape):
            return nc.dram_tensor(name, shape, F32).ap()

        toep = dram("toep", [H * P * RV])
        mgate = dram("mgate", [2 * DC, P, T])
        gscr = dram("gscr", [6, NP_, DEC_S, DEC_B])

        raw = sbuf(ctx, "raw", [P, RAW_SLOTS, UNIT])
        whi = [sbuf(ctx, f"whi{e}", [P, UNIT], F32R) for e in range(2)]
        wlo = [sbuf(ctx, f"wlo{e}", [P, UNIT], F32R) for e in range(2)]
        xhi = sbuf(ctx, "xhi", [P, DC, T], F32R)
        xlo = sbuf(ctx, "xlo", [P, DC, T], F32R)
        ada = sbuf(ctx, "ada", [P, NADA, NSEQ])
        bada = sbuf(ctx, "bada", [P, NADA])
        condp = sbuf(ctx, "condp", [P, DC, 32])
        adp = sbuf(ctx, "adp", [P, 2, P])
        selq = sbuf(ctx, "selq", [P, NSEQ])
        lnp = sbuf(ctx, "lnp", [P, 2, 2, DC])
        ones = sbuf(ctx, "ones", [P, P])
        epst = sbuf(ctx, "epst", [P, 1])
        ident = sbuf(ctx, "ident", [P, P])
        bank = [ctx.enter_context(nc.psum_tensor(f"bank{b}", [P, 512], F32)) for b in range(8)]

        pz = ExitStack()
        oh = sbuf(pz, "oh", [33, 512])
        ohr = sbuf(pz, "ohr", [33, 392])
        rel1 = sbuf(pz, "rel1", [33, H])
        selt = sbuf(pz, "selt", [33, DEC_S, P])
        rrow = sbuf(pz, "rrow", [H, RV])
        pz.close()
        s1 = ExitStack()
        qT = sbuf(s1, "qT", [P, NP_, T])
        kvT = sbuf(s1, "kvT", [P, 3, 4, T])
        kcT = sbuf(s1, "kcT", [P, 2, NSEQ, NCMP])
        hv = sbuf(s1, "hv", [P, 2, NSEQ, NCMP])
        vtok = sbuf(s1, "vtok", [P, 2, 512])
        vcp = sbuf(s1, "vcp", [NCMP, 256])
        gtok = sbuf(s1, "gtok", [P, 2, 6 * NP_])
        gs = sbuf(s1, "gs", [P, DEC_B, 3])
        w2b = sbuf(s1, "w2b", [P, 2, P])
        biasC = sbuf(s1, "biasC", [P, 2, NCMP, H])
        biasS = sbuf(s1, "biasS", [P, PAST + DEC_S])
        biasCS = sbuf(s1, "biasCS", [P, NCMP])
        maskC = sbuf(s1, "maskC", [P, 2, NCMP])
        yv = sbuf(s1, "yv", [P, RC, T])
        btanh = sbuf(s1, "btanh", [P, 2 * DC])
        cstash = sbuf(s1, "cstash", [P, RC, NSEQ, 3])
        hstash = sbuf(s1, "hstash", [P, RC, NSEQ])
        ptab = sbuf(s1, "ptab", [1, 2 * DEC_B], I32)
        p0 = ExitStack()
        xt = sbuf(p0, "xt", [P, DC, T])
        xm = sbuf(p0, "xm", [P, 2, 4, T])
        p0.close()
        p1 = ExitStack()
        cmp_rows = sbuf(p1, "cmp_rows", [P, 2 * NSEQ + 1, PAST])
        rxp = sbuf(p1, "rxp", [P, LPAD])
        gy = sbuf(p1, "gy", [P, T])
        xc = sbuf(p1, "xc", [P, LPAD])
        rg = sbuf(p1, "rg", [P, LPAD])
        ig = sbuf(p1, "ig", [P, LPAD])
        th = sbuf(p1, "th", [P, LPAD])
        av = sbuf(p1, "av", [P, LPAD])
        hk = sbuf(p1, "hk", [P, 2 * NSEQ * NCMP])
        w1d = sbuf(p1, "w1d", [P, CMP, HD])
        gT = sbuf(p1, "gT", [6 * NP_, T])
        gTs = sbuf(p1, "gTs", [6 * NP_, TS])
        cond = sbuf(p1, "cond", [P, DC, NSEQ])
        graw = sbuf(p1, "graw", [P, DC, 6 * NP_])
        qb = sbuf(p1, "qb", [P, NP_])
        kvb = sbuf(p1, "kvb", [P, 3, 4])
        gb = sbuf(p1, "gb", [6 * NP_, 1])
        rb = sbuf(p1, "rb", [P, 2, RC])
        wad = sbuf(p1, "wad", [P, 2, RC, P])
        convw = sbuf(p1, "convw", [P, 4, RC])
        lrup = sbuf(p1, "lrup", [P, 4, RC])
        sp = sbuf(p1, "sp", [P, 6, RC])
        cst = sbuf(p1, "cst", [P, RC, DEC_B, 3])
        h0t = sbuf(p1, "h0t", [P, RC, DEC_B])
        ah = sbuf(p1, "ah", [P, DEC_B])
        wcur = sbuf(p1, "wcur", [P, 2, P])
        cbias = sbuf(p1, "cbias", [P, 1])
        p1.close()
        p2 = ExitStack()
        bz = sbuf(p2, "bz", [P, 2, PAST])
        qz = sbuf(p2, "qz", [P, 2, TP])
        qzs = sbuf(p2, "qzs", [P, KVH, 32])
        ks = sbuf(p2, "ks", [P, 2, 2, PAST + DEC_S])
        vs = sbuf(p2, "vs", [P, 2, 2, 256])
        vn = sbuf(p2, "vn", [P, 2, 2, DEC_S])
        vnew = sbuf(p2, "vnew", [DEC_S, 512])
        kcs = sbuf(p2, "kcs", [P, 2, NCMP])
        hvs = sbuf(p2, "hvs", [P, 2, NCMP])
        vcs = sbuf(p2, "vcs", [NCMP, 256])
        pb = sbuf(p2, "pb", [P, 3, 512])
        pcs = sbuf(p2, "pcs", [P, 4, NCMP])
        pss = sbuf(p2, "pss", [P, 2, PAST + DEC_S])
        pcc = sbuf(p2, "pcc", [P, NCMP])
        pT = sbuf(p2, "pT", [P, 3, 512])
        pcT = sbuf(p2, "pcT", [NCMP, 512])
        psT = sbuf(p2, "psT", [P, 512])
        psn = sbuf(p2, "psn", [DEC_S, 256])
        psc = sbuf(p2, "psc", [NCMP, P])
        st = sbuf(p2, "st", [P, 4, 12])
        stc = sbuf(p2, "stc", [P, 3, 4])
        mg = sbuf(p2, "mg", [P, 2, T])
        p2.close()
        p3 = ExitStack()
        ohi = sbuf(p3, "ohi", [P, NP_, T], F32R)
        olo = sbuf(p3, "olo", [P, NP_, T], F32R)
        yhi = sbuf(p3, "yhi", [P, RC, T], F32R)
        ylo = sbuf(p3, "ylo", [P, RC, T], F32R)
        mgl = sbuf(p3, "mgl", [P, 2, 2, T])
        mt = sbuf(p3, "mt", [P, 2, T])
        p3.close()
        s1.close()
        s2 = ExitStack()
        z = sbuf(s2, "z", [P, DC, T])
        hhi = sbuf(s2, "hhi", [P, HALF, T], F32R)
        hlo = sbuf(s2, "hlo", [P, HALF, T], F32R)
        ht = sbuf(s2, "ht", [P, 2, T])
        zt = sbuf(s2, "zt", [P, T])
        mean = sbuf(s2, "mean", [P, T])
        rstd = sbuf(s2, "rstd", [P, T])
        sq = sbuf(s2, "sq", [P, 2, 4, T])
        s2.close()

        raw_in = [sem(f"raw_in{s}") for s in range(RAW_SLOTS)]
        raw_used = [sem(f"raw_used{s}") for s in range(RAW_SLOTS)]
        hi_done = sem("hi_done")
        glo_done = sem("glo_done")
        unit_done = sem("unit_done")
        acc_free = [sem("acc_free0"), sem("acc_free1")]
        ada_cp = sem("ada_cp")
        ada_t = sem("ada_t")
        ada_out = sem("ada_out")
        c_in, x_in, w_in_s, z_in = sem("c_in"), sem("x_in"), sem("w_in_s"), sem("z_in")
        b_in, pt_in = sem("b_in"), sem("pt_in")
        pool_set, dve_set, act_set = sem("pool_set"), sem("dve_set"), sem("act_set")
        cond_ok, bias_mm, bias_ok = sem("cond_ok"), sem("bias_mm"), sem("bias_ok")
        toep_out, toep_in = sem("toep_out"), sem("toep_in")
        mod_f, mod_hi, mod_lo = sem("mod_f"), sem("mod_hi"), sem("mod_lo")
        gate_t, gt_ok = sem("gate_t"), sem("gt_ok")
        g_out, g_in = sem("g_out"), sem("g_in")
        vt_mm, vt_ok = sem("vt_mm"), sem("vt_ok")
        rows_in, rows_cp, w1_in, cmp_mm, cmp_act = sem("rows_in"), sem("rows_cp"), [sem("w1k_in"), sem("w1v_in")], sem("cmp_mm"), sem("cmp_act")
        w2_mm, kc_ok = sem("w2_mm"), sem("kc_ok")
        st_pre, st_conv = sem("st_pre"), sem("st_conv")
        conv_ok, rgate_mm, rg_act, q_ok, sq_ok, y_ok = (sem(n) for n in (
            "conv_ok", "rgate_mm", "rg_act", "q_ok", "sq_ok", "y_ok"))
        gy_ok, wc_ok = sem("gy_ok"), sem("wc_ok")
        bz_in, k_in, v_in, staged, scored, extra_mm, extra_ok = (sem(n) for n in (
            "bz_in", "k_in", "v_in", "staged", "scored", "extra_mm", "extra_ok"))
        s_read, exped, p_ok, pt_mm, pt_act, pt_dve, pv_mm, o_ok = (sem(n) for n in (
            "s_read", "exped", "p_ok", "pt_mm", "pt_act", "pt_dve", "pv_mm", "o_ok"))
        mg_out, mgl_in = [sem("mg_out0"), sem("mg_out1")], [sem("mgl_in0"), sem("mgl_in1")]
        osp_hi, osp_lo, m_add, m_hi, m_ok = sem("osp_hi"), sem("osp_lo"), sem("m_add"), sem("m_hi"), sem("m_ok")
        z_ok, ln_mean, ln_c, ln_sq, ln_var, ln_std, ln_n, ln_out = (sem(n) for n in (
            "z_ok", "ln_mean", "ln_c", "ln_sq", "ln_var", "ln_std", "ln_n", "ln_out"))
        h_hi, h_lo = sem("h_hi"), sem("h_lo")
        stored, y_out = sem("stored"), sem("y_out")
        dve_c, pool_c, act_c = sem("dve_c"), sem("pool_c"), sem("act_c")

        def f32(ap):
            return ap.bitcast(F32)

        def split_hi(act, st_, i, j, size=UNIT):
            s, k = st_.rawG(i, j)
            e = (st_.g0 + j) % 2
            act.wait_ge(raw_in[s], k * 16 + 16)
            act.wait_ge(unit_done, st_.g(i, j) - 1)
            nc.scalar.copy(whi[e][:, 0:size], raw[:, s, 0:size]).then_inc(hi_done, 1)

        def split_lo(dve, st_, i, j, size=UNIT):
            s, k = st_.rawG(i, j)
            e = (st_.g0 + j) % 2
            dve.wait_ge(hi_done, st_.g(i, j) + 1)
            nc.vector.tensor_tensor(wlo[e][:, 0:size], raw[:, s, 0:size], f32(whi[e][:, 0:size]),
                                    ALU.subtract).then_inc(raw_used[s], 1)

        def after(eng, s_, value):
            if not (isinstance(value, int) and value < 1):
                eng.wait_ge(s_, value)

        def steps(eng, n, body):
            body(0)
            with eng.Fori(1, n) as i:
                body(i)

        def read_out(eng, o0, i, per, j):
            eng.wait_ge(acc_free[(o0 + j) % 2], i * (per // 2) + ((o0 + j) // 2 + 1))

        def kv_written(eng):
            read_out(eng, KVS.g0, KVS.n - 1, 4, 3)


        def bc(ap, n):
            ap = ap.unsqueeze(len(ap.shape))
            return ap.broadcast_to(list(ap.shape[:-1]) + [n])

        def starts(t, n, first=S0):
            return t[:, first:first + 7 * DEC_B].rearrange("p (b s) -> p b s", s=7)[:, :, 0:n]

        def grp(t, c0, n):
            return t[:, c0:c0 + n, TP:T].rearrange("p c (b s) -> p c b s", s=DEC_S)

        block = ctx.enter_context(nc.Block())
        N_SMALL = 19
        SMALL = 16 * N_SMALL
        N_POOL = 10

        @block.sync
        def _(sp):
            def load(st_, i, pos, first=False):
                s, k = st_.raw(i, pos)
                if not first:
                    sp.wait_ge(raw_used[s], k)
                if st_ in FOUT:
                    r = i * st_.U + (pos + st_.n * st_.U * FOUT.index(st_))
                    sp.dma_start(raw[:, s, 0:KUNIT], a["w_ffn_out_units"][r]).then_inc(raw_in[s], 16)
                else:
                    r0 = st_.r0 - (FOUT[0].n * FOUT[0].U if st_ is FIN[1] else 0)
                    sp.dma_start(raw[:, s], a["w_units"][i * st_.U + (r0 + pos)]).then_inc(raw_in[s], 16)

            for pos in range(RAW_SLOTS):
                load(INIT, 0, pos, first=True)
            with sp.Fori(1, INIT.n) as i:
                for pos in range(INIT.U):
                    load(INIT, i, pos)
            for st_ in (QS, KVS, RNN, MRG, CMB, OUT, FIN[0], FOUT[0], FIN[1], FOUT[1]):
                with sp.Fori(0, st_.n) as i:
                    for pos in range(st_.U):
                        load(st_, i, pos)
            for q in range(4):
                sp.wait_ge(ln_out, 16 + 4 * q + 4)
                sp.dma_start(out["y"][:, 4 * q:4 * q + 4, :], z[:, 4 * q:4 * q + 4, :]).then_inc(y_out, 16)
            sp.wait_ge(y_out, 16 * 4)
            sp.wait_ge(stored, 16 * 3)

        @block.gpsimd
        def _(pool):
            def one(ins, s_, value):
                ins.then_inc(s_, 1)
                pool.wait_ge(s_, value)

            for n, (dst, v) in enumerate(((condp, 0.0), (f32(whi[0][:]), 0.0), (f32(wlo[0][:]), 0.0), (selt, 0.0), (rel1[32:33, :], 1.0),
                           (w2b, 0.0), (wad, 0.0), (ones, 1.0 / D), (epst, EPS), (gs, 0.0))):
                one(pool.memset(dst if isinstance(dst, bass.AP) else dst[:], v), pool_set, n + 1)
            for h in range(2):
                half = slice(64 * h, 64 * h + 64)
                pool.dma_start(w2b[half, :, half], a["cmp_w2"].rearrange("k d e -> d k e")).then_inc(w_in_s, 16)
                for w, name in enumerate(("lru_wa", "lru_wi")):
                    pool.dma_start(wad[half, w, :, half],
                                   a[name].rearrange("(c a) d e -> a d c e", a=2)[h]).then_inc(w_in_s, 16)
            pool.wait_ge(bias_ok, 1)
            pool.dma_start(toep.rearrange("(h p y) -> h p y", h=H, p=P),
                           rrow[:].unsqueeze(1).broadcast_to([H, P, RV])).then_inc(toep_out, 16)
            pool.wait_ge(mod_lo, 4)
            one(pool.memset(rxp[:, 0:3], 0.0), st_pre, 1)
            one(pool.memset(cmp_rows[:, 2 * NSEQ, CMP:PAST], 0.0), rows_cp, 1)

            def load_rows(kv):
                seqs = cmp_rows[:, 0:2 * NSEQ].rearrange("p (g s) t -> p g s t", s=NSEQ)
                pool.dma_start(cmp_rows[:, 2 * NSEQ, 0:CMP], a["cmp_pos"][kv]).then_inc(rows_in, 16)
                with pool.Fori(0, DEC_B) as b:
                    for pg in range(2):
                        page = pool.value_load(ptab[0:1, bass.ds(b * 2 + pg, 1)], min_val=0, max_val=a["n_phys"] - 1)
                        pool.dma_start(seqs[:, :, bass.ds(b, 1), pg * PAGE:(pg + 1) * PAGE],
                                       a["cmp_k" if kv == 0 else "cmp_v"][page].unsqueeze(2)).then_inc(rows_in, 16)
                kv_written(pool)
                one(pool.tensor_copy(seqs[:, :, DEC_B, :], kvT[:, 0, 2 * kv:2 * kv + 2, 0:TP]), rows_cp, 2 + kv)

            pool.wait_ge(b_in, SMALL)
            load_rows(0)
            read_out(pool, 0, 0, 2, 0)
            pool.tensor_copy(gTs[:].rearrange("c (s b) -> c s b", s=DEC_S),
                             gT[:, TP:T].rearrange("c (b s) -> c s b", s=DEC_S)).then_inc(pool_c, 1)
            pool.wait_ge(pool_c, 1)
            with nc.allow_non_contiguous_dma(reason="1536 gates, once"):
                for m in range(6):
                    pool.dma_start(gscr[m].rearrange("c s b -> c (s b)"), gTs[m:48:6, :]).then_inc(g_out, 16)
                pool.wait_ge(g_out, 16 * 6)
                for g in range(KVH):
                    for k in range(3):
                        rows = gscr[(g % 2) * 3 + k, 4 * (g // 2):4 * (g // 2) + 4].rearrange("r s b -> (r s) b")
                        pool.dma_start(gs[32 * g:32 * g + 16, :, k], rows).then_inc(g_in, 16)
            def conv_states(i):
                for cc in range(2):
                    c = i * 2 + cc
                    after(pool, rgate_mm, c)
                    one(pool.tensor_copy(wcur[:], wad[:, :, bass.ds(c, 1), :].squeeze(2)), wc_ok, c + 1)
                    after(pool, conv_ok, c)
                    after(pool, st_conv, c)
                    one(pool.tensor_copy(starts(rxp, 3, TP + 3), cst[:, bass.ds(c, 1)].squeeze(1)), st_pre, c + 2)
                    read_out(pool, RNN.g0, i, 4, 2 * cc)
                    one(pool.tensor_copy(cstash[:, bass.ds(c, 1), 0, :].squeeze(1), rxp[:, TP:TP + 3]), pool_c, c + 2)
                    one(pool.tensor_copy(cstash[:, bass.ds(c, 1), 1:NSEQ, :].squeeze(1),
                                         starts(rxp, 7, TP + 3)[:, :, 4:7]), st_conv, c + 1)
            steps(pool, RNN.n, conv_states)
            pool.wait_ge(cmp_mm, 1)
            pool.dma_start(w1d[:], a["cmp_w1"][1]).then_inc(w1_in[1], 16)
            load_rows(1)
            pool.dma_start(out["kv"], kvT[:]).then_inc(stored, 16)
            pool.wait_ge(pool_c, 9)
            pool.wait_ge(st_conv, 8)
            pool.wait_ge(y_ok, 8)
            pool.dma_start(out["conv"], cstash[:]).then_inc(stored, 16)
            pool.dma_start(out["h"], hstash[:]).then_inc(stored, 16)
            pool.wait_ge(w2_mm, 2)
            pool.wait_ge(kc_ok, 3)
            one(pool.memset(qz[:], 0.0), st_pre, 10)
            one(pool.memset(qzs[:], 0.0), st_pre, 11)
            pool.wait_ge(toep_out, 16)
            pool.wait_ge(g_in, 16 * 12)

            def load_keys(t):
                for h in range(2):
                    src = toep[bass.ds((t * 2 + h) * (P * RV) + (P - 1), P * (RV - 1))].rearrange("(p y) -> p y", y=RV - 1)
                    pool.dma_start(bz[:, h], src[:, 0:PAST]).then_inc(bz_in, 16)
                for pg in range(2):
                    page = pool.value_load(ptab[0:1, bass.ds(t * 2 + pg, 1)], min_val=0, max_val=a["n_phys"] - 1)
                    pool.dma_start(ks[:, 0, :, pg * PAGE:(pg + 1) * PAGE], a["slc_k"][page]).then_inc(k_in, 16)
                pool.dma_start(ks[:, 1, :, 0:PAST], a["win_k"][t]).then_inc(k_in, 16)

            def load_values(t):
                pool.dma_start(vs[:, 1, :, :], a["win_v"][t]).then_inc(v_in, 16)
                for pg in range(2):
                    page = pool.value_load(ptab[0:1, bass.ds(t * 2 + pg, 1)], min_val=0, max_val=a["n_phys"] - 1)
                    pool.dma_start(vs[:, 0, pg, :], a["slc_v"][page]).then_inc(v_in, 16)

            def attend(i, g2, more):
                t = i + 4 * g2
                after(pool, scored, t * 3)
                after(pool, extra_mm, t)
                for h in range(2):
                    half = slice(64 * h, 64 * h + 64)
                    one(pool.tensor_copy(qz[half, h, :], qT[half, bass.ds(t, 1), 0:TP].squeeze(1)), staged, t * 8 + (2 * h + 1))
                    one(pool.tensor_copy(qzs[half, h:KVH:2, 0:16].rearrange("p g (r s) -> p g r s", s=DEC_S),
                                         qT[half, :, bass.ds(t * DEC_S + TP, DEC_S)].rearrange("p (g r) s -> p g r s", r=4)),
                        staged, t * 8 + (2 * h + 2))
                one(pool.tensor_copy(ks[:, :, :, PAST:PAST + DEC_S], kvT[:, 1:3, 0:2, bass.ds(t * DEC_S + TP, DEC_S)]),
                    staged, t * 8 + 5)
                one(pool.tensor_copy(vn[:], kvT[:, 1:3, 2:4, bass.ds(t * DEC_S + TP, DEC_S)]), staged, t * 8 + 6)
                one(pool.tensor_copy(kcs[:], kcT[:, :, bass.ds(t, 1), :].squeeze(2)), staged, t * 8 + 7)
                one(pool.tensor_copy(hvs[:], hv[:, :, bass.ds(t, 1), :].squeeze(2)), staged, t * 8 + 8)
                for j in range(4):
                    if j == 3 and more:
                        pool.wait_ge(pv_mm, t + 1)
                    read_out(pool, MRG.g0, t, 4, j)
                    pool.dma_start(mgate[t * 4 + j], mg[:, j % 2]).then_inc(mg_out[j % 2], 16)
                    if j == 0 and more:
                        pool.wait_ge(scored, t * 3 + 3)
                        pool.wait_ge(s_read, t * 3 + 3)
                        load_keys(t + 1)
                if more:
                    load_values(t + 1)

            load_keys(0)
            load_values(0)
            steps(pool, 4, lambda i: attend(i, 0, True))
            with pool.Fori(0, 3) as i:
                attend(i, 1, True)
            attend(3, 1, False)
            pool.wait_ge(mg_out[0], 16 * 16)
            pool.wait_ge(mg_out[1], 16 * 16)
            pool.wait_ge(o_ok, 16)
            src = mgate.rearrange("(k n) p t -> n p k t", k=2)
            for n in range(2):
                pool.dma_start(mgl[:, n], src[n]).then_inc(mgl_in[n], 16)
            with pool.Fori(1, DC // 2) as i:
                for n in range(2):
                    pool.wait_ge(m_add, i * 2 + (n - 1))
                    pool.dma_start(mgl[:, n], src[i * 2 + n]).then_inc(mgl_in[n], 16)
            pool.wait_ge(m_ok, DC)
            pool.wait_ge(unit_done, CMB.g_end)
            pool.wait_ge(stored, 48)
            pool.dma_start(z[:], a["x"]).then_inc(z_in, 16)

        @block.tensor
        def _(pe):
            def g_unit(st_, i, j, kin, parts, done=True):
                s, k = st_.rawG(i, j)
                e = (st_.g0 + j) % 2
                pe.wait_ge(raw_used[s], k + 1)
                three(e, kin, parts).then_inc(unit_done, 1)

            def three(e, kin, parts):
                for b, k0, mh, ml, c0, start, stop in parts:
                    for kk in range(kin):
                        w = slice((k0 + kk) * P, (k0 + kk + 1) * P)
                        acc = bank[b][:, 0:T]
                        pe.matmul(acc, wlo[e][:, w], mh[:, c0 + kk, :], start=start and kk == 0, stop=False)
                        pe.matmul(acc, whi[e][:, w], ml[:, c0 + kk, :], start=False, stop=False)
                        m = pe.matmul(acc, whi[e][:, w], mh[:, c0 + kk, :], start=False, stop=stop and kk == kin - 1)
                return m

            def a_pair(st_, i, m):
                for e in range(2):
                    s, k = st_.raw(i, st_.A[2 * m + e])
                    pe.wait_ge(raw_in[s], k * 16 + 16)
                    for kk in range(4):
                        for q in range(4):
                            c = 4 * q + kk
                            ins = pe.matmul(bank[6 + e][32 * q:32 * q + 32, 0:P], condp[:, c, :],
                                            raw[:, s, c * P:(c + 1) * P], start=kk == 0, stop=kk == 3)
                    ins.then_inc(raw_used[s], 1)

            def a_turn(q):
                pe.wait_ge(ada_cp, q + 1)
                after(pe, ada_out, q)
                for e in range(2):
                    ins = pe.matmul(bank[4][:, 16 * e:16 * e + NSEQ], adp[:, e, :], selq[:], start=True, stop=True)
                ins.then_inc(ada_t, 1)

            def pairs(st_, i, m):
                return i * (len(st_.A) // 2) + (st_.a0 // 2 + m)

            def free(o):
                pe.wait_ge(acc_free[o % 2 if isinstance(o, int) else 0], o // 2)

            pe.wait_ge(b_in, SMALL)
            pe.wait_ge(pool_set, N_POOL)
            pe.wait_ge(w_in_s, 16 * 6)
            pe.wait_ge(dve_set, 1)
            pe.matmul(bank[0][0:H, 0:RV], rel1[:], ohr[:, 4:4 + RV], start=True, stop=True)
            for qt in range(2):
                for n in range(NCMP):
                    x0 = 224 + P * qt - STRIDE * n
                    pe.matmul(bank[1][:, (qt * NCMP + n) * H:(qt * NCMP + n + 1) * H], oh[:, x0:x0 + P], rel1[:],
                              start=True, stop=True)
            for s in range(DEC_S):
                pe.matmul(bank[2][:, 0:PAST + DEC_S], selt[:, s, :], ohr[:, 3 - s:3 - s + PAST + DEC_S],
                          start=s == 0, stop=s == 3)
            for s in range(DEC_S):
                ins = pe.matmul(bank[3][:, 0:NCMP], selt[:, s, :],
                                ohr[:, 34 - s:34 - s + STRIDE * NCMP:STRIDE], start=s == 0, stop=s == 3)
            ins.then_inc(bias_mm, 1)

            pe.wait_ge(cond_ok, 1)
            def init(i):
                for m in range(2):
                    a_pair(INIT, i, m)
                    a_turn(pairs(INIT, i, m))

            steps(pe, INIT.n, init)

            X = (xhi, xlo)
            pe.wait_ge(mod_lo, 4)
            pe.wait_ge(glo_done, 1)
            pe.wait_ge(bias_ok, 1)
            three(0, DC, [(0, 0, *X, 0, True, True)]).then_inc(unit_done, 1)

            def plain(st_, i, j, o0=None):
                nG = len(st_.G)
                o = i * nG + (st_.g0 + j)
                b = (st_.g0 + j) % 2
                after(pe, acc_free[b], i * (nG // 2) + (st_.g0 + j) // 2)
                g_unit(st_, i, j, DC, [(b, 0, *X, 0, True, True)])

            def four(st_, i):
                for j in range(4):
                    plain(st_, i, j)

            steps(pe, QS.n, lambda i: four(QS, i))
            with pe.Fori(0, KVS.n) as i:
                four(KVS, i)

            read_out(pe, 0, 0, 2, 0)
            for tt in range(2):
                ins = pe.transpose(bank[5][:, tt * 48:tt * 48 + 48], gT[:, tt * P:(tt + 1) * P], ident[0:48, 0:48])
            ins.then_inc(gate_t, 1)
            kv_written(pe)
            for br in range(2):
                for tt in range(2):
                    for g2 in range(2):
                        ins = pe.transpose(bank[2 + br][:, (tt * 2 + g2) * P:(tt * 2 + g2 + 1) * P],
                                           kvT[:, 1 + br, 2 + g2, tt * P:(tt + 1) * P], ident[:])
            ins.then_inc(vt_mm, 1)

            def compress(kv):
                pe.wait_ge(w1_in[kv], 16)
                pe.wait_ge(rows_in, 16 * 17 * (kv + 1))
                pe.wait_ge(rows_cp, 2 + kv)
                pe.wait_ge(vt_ok, 1)
                after(pe, kc_ok, 2 * kv)
                after(pe, rg_act, 8 * kv)
                for l in range(CMP):
                    for h in range(2):
                        half = slice(64 * h, 64 * h + 64)
                        ins = pe.matmul(bank[2 + h][half, 0:(2 * NSEQ + 1) * NCMP], w1d[half, l, :],
                                        cmp_rows[half, :, l:l + STRIDE * (NCMP - 1) + 1:STRIDE], start=l == 0, stop=l == CMP - 1)
                ins.then_inc(cmp_mm, 1)

            def compress_out(kv):
                pe.wait_ge(cmp_act, kv + 1)
                if kv == 0:
                    pe.matmul(bank[2][:, 0:2 * NSEQ * NCMP], w2b[:, 0, :], hk[:], start=True, stop=True).then_inc(w2_mm, 1)
                else:
                    for g2 in range(2):
                        ins = pe.matmul(bank[3][0:NCMP, g2 * P:(g2 + 1) * P], hv[:, g2, DEC_B, :], w2b[:, 1, :],
                                        start=True, stop=True)
                    ins.then_inc(w2_mm, 1)

            compress(0)
            compress_out(0)

            def recurrent(i):
                for j in range(4):
                    plain(RNN, i, j)
                    if j:
                        a_turn(pairs(RNN, i, j - 1))
                    a_pair(RNN, i, j)
                    if j == 3:
                        a_turn(pairs(RNN, i, 3))
                    if j % 2:
                        c = i * 2 + j // 2
                        pe.wait_ge(conv_ok, c + 1)
                        pe.wait_ge(wc_ok, c + 1)
                        after(pe, rg_act, c)
                        if j == 1:
                            pe.wait_ge(kc_ok, 1)
                        for w in range(2):
                            ins = pe.matmul(bank[2 + w][:, 0:L], wcur[:, w, :], xc[:, 0:L], start=True, stop=True)
                        ins.then_inc(rgate_mm, 1)
            steps(pe, RNN.n, recurrent)
            compress(1)
            compress_out(1)
            pe.wait_ge(kc_ok, 3)

            def attend(i, g2):
                t = i + 4 * g2
                i8 = t

                def unit(j):
                    b = (MRG.g0 + j) % 2
                    pe.wait_ge(acc_free[b], i8 * 2 + (MRG.g0 + j) // 2)
                    g_unit(MRG, i8, j, DC, [(b, 0, *X, 0, True, True)])

                unit(0)
                pe.wait_ge(staged, t * 8 + 8)
                for h in range(2):
                    for br in range(2):
                        pe.matmul(bank[4][:, (h * 2 + br) * P:(h * 2 + br + 1) * P], qz[:, h, 0:P],
                                  kvT[:, 1 + br, g2, 0:P], start=True, stop=True)
                for qt in range(2):
                    for h in range(2):
                        c = (qt * 2 + h) * NCMP
                        ins = pe.matmul(bank[5][:, c:c + NCMP], qz[:, h, qt * P:(qt + 1) * P], kcT[:, g2, DEC_B, :],
                                        start=True, stop=True)
                ins.then_inc(scored, 1)
                after(pe, o_ok, t * 2)
                for h in range(2):
                    for br in range(2):
                        ins = pe.matmul(bank[2 + h][:, br * TP:(br + 1) * TP], qz[:, h, P:TP],
                                        kvT[:, 1 + br, g2, 0:TP], start=True, stop=True)
                ins.then_inc(scored, 1)
                pe.wait_ge(k_in, t * 48 + 48)
                for br in range(2):
                    for g in range(KVH):
                        pe.matmul(bank[6 + br][32 * g:32 * g + 32, 0:PAST + DEC_S], qzs[:, g, :], ks[:, br, g // 2, :],
                                  start=True, stop=True)
                for g in range(KVH):
                    ins = pe.matmul(bank[6][32 * g:32 * g + 32, 264:264 + NCMP], qzs[:, g, :], kcs[:, g // 2, :],
                                    start=True, stop=True)
                ins.then_inc(scored, 1)
                unit(1)
                pe.wait_ge(s_read, t * 3 + 1)
                for br in range(2):
                    for g in range(2):
                        pe.transpose(bank[4][0:DEC_S, (br * 2 + g) * P:(br * 2 + g + 1) * P], vn[:, br, g, :], ident[:])
                for g in range(2):
                    ins = pe.matmul(bank[5][0:NCMP, g * P:(g + 1) * P], hvs[:, g, :], w2b[:, 1, :], start=True, stop=True)
                ins.then_inc(extra_mm, 1)
                unit(2)
                pe.wait_ge(p_ok, t * 3 + 1)
                pe.wait_ge(extra_ok, t + 1)
                for c in range(4):
                    pe.transpose(bank[4][:, c * P:(c + 1) * P], pb[:, 0, c * P:(c + 1) * P], ident[:])
                for c in range(4):
                    ins = pe.transpose(bank[5][0:NCMP, c * P:(c + 1) * P], pcs[:, c, :], ident[:])
                ins.then_inc(pt_mm, 1)
                pe.wait_ge(p_ok, t * 3 + 2)
                pe.wait_ge(s_read, t * 3 + 3)
                for h in range(2):
                    for c in range(4):
                        ins = pe.transpose(bank[2 + h][:, c * P:(c + 1) * P], pb[:, 1 + h, c * P:(c + 1) * P], ident[:])
                ins.then_inc(pt_mm, 1)
                pe.wait_ge(p_ok, t * 3 + 3)
                for c in range(4):
                    pe.transpose(bank[6][:, c * P:(c + 1) * P], pss[:, c // 2, (c % 2) * P:(c % 2 + 1) * P], ident[:])
                for br in range(2):
                    pe.transpose(bank[7][0:DEC_S, br * P:(br + 1) * P], pss[:, br, PAST:PAST + DEC_S], ident[:])
                pe.transpose(bank[7][0:NCMP, 2 * P:3 * P], pcc[:], ident[:]).then_inc(pt_mm, 1)
                unit(3)
                pe.wait_ge(pt_act, t * 3 + 3)
                pe.wait_ge(pt_dve, t + 1)
                pe.wait_ge(v_in, t * 48 + 48)
                for h in range(2):
                    dims = slice(g2 * P + 64 * h, g2 * P + 64 * h + 64)
                    for qt in range(2):
                        o_ = bank[2][64 * h:64 * h + 64, qt * P:(qt + 1) * P]
                        pe.matmul(o_, vcp[:, dims], pcT[:, (qt * 2 + h) * P:(qt * 2 + h + 1) * P], start=True, stop=False)
                        todo = [(br, kt) for br in range(2) for kt in range(qt + 1)]
                        for n, (br, kt) in enumerate(todo):
                            p_ = pT[:, 0, (h * 2 + br) * P:(h * 2 + br + 1) * P] if qt == 0 else \
                                pT[:, 1 + h, (br * 2 + kt) * P:(br * 2 + kt + 1) * P]
                            v0 = kt * 256 + dims.start
                            pe.matmul(o_, vtok[:, br, v0:v0 + 64], p_, start=False, stop=n == len(todo) - 1)
                for g in range(KVH):
                    o_ = bank[3][64 * (g % 2):64 * (g % 2) + 64, (g // 2) * 16:(g // 2) * 16 + 16]
                    dims = slice(64 * g, 64 * g + 64)
                    pe.matmul(o_, vcs[:, dims], psc[:, 32 * g:32 * g + 16], start=True, stop=False)
                    for br in range(2):
                        pe.matmul(o_, vnew[:, br * 256 + dims.start:br * 256 + dims.stop],
                                  psn[:, br * P + 32 * g:br * P + 32 * g + 16], start=False, stop=False)
                    for br in range(2):
                        for kt in range(2):
                            ins = pe.matmul(o_, vs[:, br, kt, dims], psT[:, (br * 2 + kt) * P + 32 * g:(br * 2 + kt) * P + 32 * g + 16],
                                            start=False, stop=br == 1 and kt == 1)
                ins.then_inc(pv_mm, 1)

            steps(pe, 4, lambda i: attend(i, 0))
            with pe.Fori(0, 4) as i:
                attend(i, 1)

            pe.wait_ge(osp_lo, 2)
            pe.wait_ge(o_ok, 16)
            with pe.Fori(0, CMB.n) as i:
                for j in range(4):
                    b = (CMB.g0 + j) % 2
                    pe.wait_ge(acc_free[b], i * 2 + (CMB.g0 + j) // 2)
                    g_unit(CMB, i, j, RC, [(b, 0, ohi, olo, 0, True, True), (2 + b, RC, yhi, ylo, 0, True, True)])
                    if j % 2 == 0:
                        a_pair(CMB, i, j // 2)
                    else:
                        a_turn(pairs(CMB, i, j // 2))
            pe.wait_ge(m_ok, DC)
            with pe.Fori(0, OUT.n) as i:
                for j in range(4):
                    plain(OUT, i, j)
                    if j % 2 == 0:
                        a_pair(OUT, i, j // 2)
                    else:
                        a_turn(pairs(OUT, i, j // 2))

            def norm(n):
                pe.wait_ge(z_ok, 16 if n == 0 else 48)
                for c in range(DC):
                    ins = pe.matmul(bank[2][:, 0:T], ones[:], z[:, c, :], start=c == 0, stop=c == DC - 1)
                ins.then_inc(ln_mean, 1)
                for q in range(4):
                    pe.wait_ge(ln_sq, 4 * n + q + 1)
                    for c in range(4):
                        ins = pe.matmul(bank[3][:, 0:T], ones[:], sq[:, q % 2, c, :], start=q == 0 and c == 0,
                                        stop=q == 3 and c == 3)
                    ins.then_inc(ln_var, 1)

            norm(0)
            pe.wait_ge(mod_lo, 8)
            for half in range(2):
                st_, o0 = FIN[half], O_FIN[half]

                def fin(i):
                    for j in range(4):
                        b = (o0 + j) % 2
                        pe.wait_ge(acc_free[b], i * 2 + (o0 + j) // 2)
                        g_unit(FIN[half], i, j, DC, [(b, 0, *X, 0, True, True)])

                with pe.Fori(0, st_.n) as i:
                    fin(i)
                pe.wait_ge(h_lo, HALF * (half + 1))
                o0 = O_FOUT[half]
                with pe.Fori(0, FOUT[half].n) as i:
                    for j in range(4):
                        b = (O_FOUT[half] + j // 2) % 2
                        if j % 2 == 0:
                            pe.wait_ge(acc_free[b], i + (O_FOUT[half] + j // 2) // 2)
                        g_unit(FOUT[half], i, j, KS, [(b, 0, hhi, hlo, KS * (j % 2), j % 2 == 0, j % 2 == 1)])
            norm(1)

        @block.scalar
        def _(act):
            act.dma_start(cond[:], a["cond"]).then_inc(c_in, 16)
            act.dma_start(xt[:], a["x"]).then_inc(x_in, 16)
            small = ((bada, "b_ada"), (lnp, "lnp"), (ident, "ident"), (selq, "selq"), (oh, "oh"), (ohr, "ohr"),
                     (rel1[0:32, :], "rel"), (maskC, "mask_c"), (graw, "w_gate"), (qb, "b_q"), (kvb, "b_kv"), (gb, "b_gate"),
                     (rb, "b_r"), (convw, "conv_w"), (lrup, "lru_p"), (cst, "conv_state"), (h0t, "rnn_h"),
                     (btanh, "b_merge"), (ptab, "page_table"))
            assert len(small) == N_SMALL
            for dst, name in small:
                act.dma_start(dst if isinstance(dst, bass.AP) else dst[:], a[name]).then_inc(b_in, 16)
            act.dma_start(w1d[:], a["cmp_w1"][0]).then_inc(w1_in[0], 16)
            act.wait_ge(c_in, 16)
            act.wait_ge(pool_set, N_POOL)
            nc.scalar.activation(condp[:, :, 0:NSEQ], cond[:], ACT.Silu).then_inc(cond_ok, 1)
            act.wait_ge(b_in, SMALL)
            act.wait_ge(dve_set, 2)
            nc.scalar.activation(sp[:, 1, :], sp[:, 0, :], ACT.Exp, scale=-1.0).then_inc(act_set, 1)

            def a_copy(st_, i, m):
                for e in range(2):
                    s, k = st_.raw(i, st_.A[2 * m + e])
                    act.wait_ge(raw_used[s], k + 1)
                    ins = nc.scalar.copy(adp[:, e, :], bank[6 + e][:, 0:P])
                ins.then_inc(ada_cp, 1)

            with act.Fori(0, INIT.n) as i:
                for m in range(2):
                    a_copy(INIT, i, m)

            def mod_high(n, tm):
                for q in range(4):
                    act.wait_ge(mod_f, 4 * n + q + 1)
                    nc.scalar.copy(xhi[:, 4 * q:4 * q + 4, :], tm[:, q % 2]).then_inc(mod_hi, 1)

            mod_high(0, xm)
            nc.scalar.copy(whi[0][:].rearrange("p (k n) -> p k n", n=P)[:, :, 0:48], graw[:]).then_inc(hi_done, 1)
            s, k = QS.rawG(0, 0)
            act.wait_ge(raw_in[s], 16 * k + 16)
            nc.scalar.copy(whi[1][:], raw[:, s]).then_inc(hi_done, 1)
            act.wait_ge(unit_done, 1)
            nc.scalar.activation(gT[:], bank[0][0:48, 0:T], ACT.Sigmoid, bias=gb[:]).then_inc(acc_free[0], 1)
            for st_ in (QS, KVS):
                with act.Fori(0, st_.n) as i:
                    for j in range(4):
                        if st_ is QS:
                            split_hi(act, st_, i, j + 1)
                        else:
                            split_hi(act, st_, i, j + 1)

            def compress_act(kv):
                act.wait_ge(cmp_mm, kv + 1)
                n = 2 * NSEQ * NCMP
                for h in range(2):
                    half = slice(64 * h, 64 * h + 64)
                    ins = nc.scalar.copy(cbias[half, :], bank[2 + h][half, n:n + 1])
                ins.then_inc(act_c, 1)
                act.wait_ge(act_c, 1 + kv * (RC + 1))
                dst = hk[:] if kv == 0 else hv[:].rearrange("p g s n -> p (g s n)")
                for h in range(2):
                    half = slice(64 * h, 64 * h + 64)
                    ins = nc.scalar.activation(dst[half, :], bank[2 + h][half, 0:n], ACT.Silu, bias=cbias[half, :])
                ins.then_inc(cmp_act, 1)
                act.wait_ge(w2_mm, kv + 1)
                if kv == 0:
                    nc.scalar.copy(kcT[:].rearrange("p g s n -> p (g s n)"), bank[2][:, 0:n]).then_inc(kc_ok, 2)
                else:
                    nc.scalar.copy(vcp[:], bank[3][0:NCMP, 0:256]).then_inc(kc_ok, 1)

            compress_act(0)
            act.wait_ge(dve_set, 3)
            def recurrent(i):
                for j in range(4):
                    c = i * 2 + j // 2
                    split_hi(act, RNN, i, j + 1)
                    if j % 2 == 0:
                        a_copy(RNN, i, j)
                        if j == 2:
                            act.wait_ge(q_ok, i * 2 + 1)
                            nc.scalar.activation(rg[:, 0:L], rg[:, 0:L], ACT.Sqrt).then_inc(sq_ok, 1)
                    else:
                        a_copy(RNN, i, j)
                        g = RNN.g(i, j)
                        act.wait_ge(unit_done, g + 1)
                        after(act, y_ok, c)
                        b = (RNN.g0 + j) % 2
                        nc.scalar.activation(gy[:], bank[b][:, 0:T], ACT.Gelu_apprx_tanh,
                                             bias=rb[:, 1, bass.ds(c, 1)]).then_inc(acc_free[b], 1)
                        act.wait_ge(rgate_mm, c + 1)
                        nc.scalar.activation(rg[:, 0:L], bank[2][:, 0:L], ACT.Sigmoid, bias=lrup[:, 1, bass.ds(c, 1)]).then_inc(act_c, 1)
                        nc.scalar.activation(ig[:, 0:L], bank[3][:, 0:L], ACT.Sigmoid, bias=lrup[:, 2, bass.ds(c, 1)]).then_inc(rg_act, 1)
                        act.wait_ge(act_c, c + 2)
                        nc.scalar.activation(th[:, 0:L], rg[:, 0:L], ACT.Tanh, scale=sp[:, 4, bass.ds(c, 1)])
                        nc.scalar.activation(av[:, 0:L], rg[:, 0:L], ACT.Exp, scale=sp[:, 5, bass.ds(c, 1)]).then_inc(gy_ok, 1)
                        if j == 3:
                            act.wait_ge(q_ok, i * 2 + 2)
                            nc.scalar.activation(rg[:, 0:L], rg[:, 0:L], ACT.Sqrt).then_inc(sq_ok, 1)
            steps(act, RNN.n, recurrent)
            compress_act(1)

            def merge_gate(t, j):
                b = (MRG.g0 + j) % 2
                act.wait_ge(unit_done, MRG.g(t, j) + 1)
                after(act, mg_out[j % 2], t * 32 + 16 * (j // 2))
                n = t * 4 + j
                nc.scalar.activation(mg[:, j % 2], bank[b][:, 0:T], ACT.Tanh, scale=0.5,
                                     bias=btanh[:, bass.ds(n, 1)]).then_inc(acc_free[b], 1)

            def attend(i, g2):
                t = i + 4 * g2

                def expo(x, col, acc=True):
                    return nc.scalar.activation(x, x, ACT.Exp, bias=st[:, 1, col:col + 1],
                                                accum_out=st[:, 2, col:col + 1])

                split_hi(act, MRG, t, 1)
                split_hi(act, MRG, t, 2)
                merge_gate(t, 0)
                act.wait_ge(s_read, t * 3 + 1)
                for c in range(4):
                    expo(pb[:, 0, c * P:(c + 1) * P], c)
                nc.scalar.activation(pcs[:], pcs[:], ACT.Exp).then_inc(exped, 1)
                act.wait_ge(s_read, t * 3 + 2)
                for c in range(4):
                    ins = expo(pb[:, 1 + c // 2, (c % 2) * TP:(c % 2 + 1) * TP], 4 + c)
                ins.then_inc(exped, 1)
                act.wait_ge(s_read, t * 3 + 3)
                expo(pss[:, 0, :], 8)
                expo(pss[:, 1, :], 9)
                expo(pcc[:], 10).then_inc(exped, 1)
                split_hi(act, MRG, t, 3)
                merge_gate(t, 1)
                act.wait_ge(extra_mm, t + 1)
                after(act, pv_mm, t)
                nc.scalar.copy(vnew[:], bank[4][0:DEC_S, :])
                nc.scalar.copy(vcs[:], bank[5][0:NCMP, 0:256]).then_inc(extra_ok, 1)
                split_hi(act, MRG, t, 4)
                merge_gate(t, 2)
                act.wait_ge(pt_mm, t * 3 + 2)
                nc.scalar.copy(pT[:, 1, :], bank[2][:])
                nc.scalar.copy(pT[:, 2, :], bank[3][:]).then_inc(pt_act, 1)
                act.wait_ge(pt_mm, t * 3 + 3)
                nc.scalar.copy(psT[:], bank[6][:]).then_inc(pt_act, 1)
                nc.scalar.copy(psn[:], bank[7][0:DEC_S, 0:2 * P])
                nc.scalar.copy(psc[:], bank[7][0:NCMP, 2 * P:3 * P]).then_inc(pt_act, 1)
                merge_gate(t, 3)

            steps(act, 4, lambda i: attend(i, 0))
            with act.Fori(0, 4) as i:
                attend(i, 1)
            act.wait_ge(o_ok, 16)
            act.wait_ge(mg_out[0], 256)
            act.wait_ge(mg_out[1], 256)
            nc.scalar.copy(ohi[:], qT[:]).then_inc(osp_hi, 1)
            nc.scalar.copy(yhi[:], yv[:]).then_inc(osp_hi, 1)
            with act.Fori(0, CMB.n) as i:
                for j in range(4):
                    n = i * 4 + j
                    split_hi(act, CMB, i, j + 1)
                    if j % 2 == 0:
                        a_copy(CMB, i, j // 2)
                    act.wait_ge(m_add, n + 1)
                    nc.scalar.activation(xhi[:, bass.ds(n, 1), :].squeeze(1), mt[:, 0, :], ACT.Copy, scale=0.5).then_inc(m_hi, 1)
            with act.Fori(0, OUT.n) as i:
                for j in range(4):
                    split_hi(act, OUT, i, j + 1)
                    if j % 2 == 0:
                        a_copy(OUT, i, j // 2)

            def norm_act(n):
                for q in range(4):
                    act.wait_ge(ln_c, 4 * n + q + 1)
                    act.wait_ge(ln_var, 4 * n + q - 1) if 4 * n + q > 1 else None
                    nc.scalar.activation(sq[:, q % 2], z[:, 4 * q:4 * q + 4, :], ACT.Square).then_inc(ln_sq, 1)
                act.wait_ge(ln_var, 4 * n + 4)
                nc.scalar.activation(rstd[:], bank[3][:, 0:T], ACT.Sqrt, bias=epst[:]).then_inc(ln_std, 1)
                for c in range(DC):
                    act.wait_ge(ln_n, 4 * n + c // 4 + 1)
                    nc.scalar.activation(z[:, c, :], z[:, c, :], ACT.Identity, scale=lnp[:, n, 0, c:c + 1],
                                         bias=lnp[:, n, 1, c:c + 1]).then_inc(ln_out, 1)

            norm_act(0)
            mod_high(1, sq)
            for half in range(2):
                def fin(i, last):
                    for j in range(4):
                        split_hi(act, FIN[half], i, j + 1, KUNIT if last and j == 3 else UNIT)
                        c = i * 2 + (j // 2 + HALF * half)
                        b = (O_FIN[half] + j) % 2
                        act.wait_ge(unit_done, FIN[half].g(i, j) + 1)
                        if j % 2 == 0:
                            act.wait_ge(h_lo, c - 1) if not (isinstance(c, int) and c < 1) else None
                            nc.scalar.activation(ht[:, j // 2], bank[b][:, 0:T], ACT.Silu).then_inc(acc_free[b], 1)
                        else:
                            read_out(act, O_FIN[half], i, 4, j)
                            nc.scalar.copy(hhi[:, bass.ds(i * 2 + j // 2, 1), :].squeeze(1), ht[:, j // 2]).then_inc(h_hi, 1)

                def fout(i, last):
                    for j in range(4):
                        if last and j == 3:
                            if half == 0:
                                split_hi(act, FOUT[half], i, j + 1, UNIT)
                        else:
                            split_hi(act, FOUT[half], i, j + 1, KUNIT)

                fin(0, False)
                with act.Fori(1, FIN[half].n - 1) as i:
                    fin(i, False)
                fin(FIN[half].n - 1, True)
                with act.Fori(0, FOUT[half].n - 1) as i:
                    fout(i, False)
                fout(FOUT[half].n - 1, True)
            norm_act(1)

        @block.vector
        def _(dve):
            ch = Chain(dve, dve_c)
            v = nc.vector
            dve.wait_ge(b_in, SMALL)
            dve.wait_ge(pool_set, N_POOL)
            v.tensor_scalar(bada[:, DC:3 * DC], bada[:, DC:3 * DC], 1.0, None, ALU.add)
            v.tensor_scalar(bada[:, 4 * DC:6 * DC], bada[:, 4 * DC:6 * DC], 1.0, None, ALU.add)
            for s in range(DEC_S):
                for h in range(2):
                    ins = v.tensor_copy(selt[:, s, :].rearrange("k (g m) -> k g m", m=32)[:, h:KVH:2, s:16:DEC_S],
                                        rel1[:].rearrange("k (g r h) -> k g r h", g=2, h=2)[:, :, :, h])
            ins.then_inc(dve_set, 1)
            v.tensor_scalar(btanh[:], btanh[:], 0.5, None, ALU.mult)
            lam = lrup[:, 3, :]
            ch(v.tensor_scalar(sp[:, 1, :], lam, -1.0, None, ALU.mult))
            v.tensor_tensor(sp[:, 0, :], lam, sp[:, 1, :], ALU.max).then_inc(dve_set, 1)
            dve.wait_ge(act_set, 1)
            e_, z_, z2, s_ = sp[:, 1, :], sp[:, 2, :], sp[:, 3, :], sp[:, 4, :]
            ch(v.tensor_scalar(z_, e_, 2.0, None, ALU.add))
            ch(v.reciprocal(z_, z_))
            ch(v.tensor_tensor(z_, z_, e_, ALU.mult))
            ch(v.tensor_tensor(z2, z_, z_, ALU.mult))
            ch(v.tensor_scalar(s_, z2, 1.0 / 15, None, ALU.mult))
            for n in (13, 11, 9, 7, 5, 3):
                ch(v.scalar_tensor_tensor(s_, s_, 1.0 / n, z2, ALU.add, ALU.mult))
            ch(v.scalar_tensor_tensor(s_, s_, 1.0, z_, ALU.add, ALU.mult))
            ch(v.tensor_scalar(e_, lam, -1.0, 0.0, ALU.mult, ALU.max))
            ch(v.scalar_tensor_tensor(s_, s_, 2.0, e_, ALU.mult, ALU.add))
            ch(v.tensor_scalar(sp[:, 5, :], s_, -LRU_C, None, ALU.mult))
            v.tensor_scalar(s_, s_, LRU_C, None, ALU.mult).then_inc(dve_set, 1)
            dve.wait_ge(bias_mm, 1)
            v.tensor_copy(rrow[:], bank[0][0:H, 0:RV])
            v.tensor_copy(biasC[:].rearrange("p q n h -> p (q n h)"), bank[1][:, 0:2 * NCMP * H])
            v.tensor_copy(biasS[:], bank[2][:, 0:PAST + DEC_S])
            v.tensor_copy(biasCS[:], bank[3][:, 0:NCMP]).then_inc(bias_ok, 1)

            def a_out(q):
                dve.wait_ge(ada_t, q + 1)
                v.tensor_tensor(ada[:, bass.ds(q * 2, 2), :], bank[4][:, 0:32].rearrange("p (e s) -> p e s", e=2)[:, :, 0:NSEQ],
                                bc(bada[:, bass.ds(q * 2, 2)], NSEQ), ALU.add).then_inc(ada_out, 1)

            def pairs(st_, i, m):
                return i * (len(st_.A) // 2) + (st_.a0 // 2 + m)

            with dve.Fori(0, INIT.n) as i:
                for m in range(2):
                    a_out(pairs(INIT, i, m))

            def modulate(n, src, tm, sh, sc):
                def low(q):
                    dve.wait_ge(mod_hi, 4 * n + q + 1)
                    v.tensor_tensor(xlo[:, 4 * q:4 * q + 4, :], tm[:, q % 2], f32(xhi[:, 4 * q:4 * q + 4, :]),
                                    ALU.subtract).then_inc(mod_lo, 1)

                for q in range(4):
                    c0 = 4 * q
                    if q >= 2:
                        low(q - 2)
                        dve.wait_ge(mod_lo, 4 * n + (q - 1))
                    for c in range(4):
                        v.tensor_scalar(tm[:, q % 2, c, 0:TP], src[:, c0 + c, 0:TP], ada[:, sc + c0 + c, 0:1],
                                        ada[:, sh + c0 + c, 0:1], ALU.mult, ALU.add)
                    new = grp(tm[:, q % 2], 0, 4)
                    ch(v.tensor_tensor(new, grp(src, c0, 4), bc(ada[:, sc + c0:sc + c0 + 4, 1:NSEQ], DEC_S), ALU.mult))
                    v.tensor_tensor(new, new, bc(ada[:, sh + c0:sh + c0 + 4, 1:NSEQ], DEC_S), ALU.add).then_inc(mod_f, 1)
                low(2)
                low(3)

            dve.wait_ge(x_in, 16)
            dve.wait_ge(ada_out, DC)
            modulate(0, xt, xm, 0, DC)
            dve.wait_ge(hi_done, 1)
            v.tensor_tensor(wlo[0][:].rearrange("p (k n) -> p k n", n=P)[:, :, 0:48], graw[:],
                            f32(whi[0][:].rearrange("p (k n) -> p k n", n=P)[:, :, 0:48]), ALU.subtract).then_inc(glo_done, 1)
            dve.wait_ge(hi_done, 2)
            s, _k = QS.rawG(0, 0)
            v.tensor_tensor(wlo[1][:], raw[:, s], f32(whi[1][:]), ALU.subtract).then_inc(raw_used[s], 1)
            dve.wait_ge(toep_out, 16)
            with dve.Fori(0, QS.n) as i:
                for j in range(4):
                    b = (QS.g0 + j) % 2
                    split_lo(dve, QS, i, j + 1)
                    dve.wait_ge(unit_done, QS.g(i, j) + 1)
                    n = i * 4 + j
                    v.tensor_scalar(qT[:, bass.ds(n, 1), :].squeeze(1), bank[b][:, 0:T], qb[:, bass.ds(n, 1)], SCALE,
                                    ALU.add, ALU.mult).then_inc(acc_free[b], 1)
            with dve.Fori(0, KVS.n) as i:
                for j in range(4):
                    b = (KVS.g0 + j) % 2
                    split_lo(dve, KVS, i, j + 1)
                    dve.wait_ge(unit_done, KVS.g(i, j) + 1)
                    v.tensor_scalar(kvT[:, bass.ds(i, 1), j, :].squeeze(1), bank[b][:, 0:T], kvb[:, bass.ds(i, 1), j],
                                    None, ALU.add).then_inc(acc_free[b], 1)
            dve.wait_ge(gate_t, 1)
            v.tensor_copy(gtok[:].rearrange("p t n -> p (t n)"), bank[5][:, 0:96]).then_inc(gt_ok, 1)
            dve.wait_ge(vt_mm, 1)
            v.tensor_copy(vtok[:, 0, :], bank[2][:])
            v.tensor_copy(vtok[:, 1, :], bank[3][:]).then_inc(vt_ok, 1)

            def chain_rnn(c):
                dve.wait_ge(gy_ok, c + 1)
                ch(v.tensor_tensor(rg[:, 0:L], av[:, 0:L], av[:, 0:L], ALU.mult))
                v.scalar_tensor_tensor(rg[:, 0:L], rg[:, 0:L], 1.0, th[:, 0:L], ALU.add, ALU.mult).then_inc(q_ok, 1)
                v.tensor_tensor(ah[:], starts(av, 1)[:, :, 0], h0t[:, bass.ds(c, 1), :].squeeze(1), ALU.mult)
                ch(v.tensor_tensor(ig[:, 0:L], ig[:, 0:L], xc[:, 0:L], ALU.mult))
                v.memset(starts(av, 1), 0.0)
                dve.wait_ge(sq_ok, c + 1)
                ch(v.tensor_tensor(rg[:, 0:L], rg[:, 0:L], ig[:, 0:L], ALU.mult))
                ch(v.tensor_tensor(starts(rg, 1)[:, :, 0], starts(rg, 1)[:, :, 0], ah[:], ALU.add))
                ch(v.tensor_tensor_scan(th[:, 0:L], av[:, 0:L], rg[:, 0:L], 0.0, ALU.mult, ALU.add))
                v.tensor_copy(hstash[:, bass.ds(c, 1), 0:1].squeeze(1), th[:, TP - 1:TP])
                v.tensor_copy(hstash[:, bass.ds(c, 1), 1:NSEQ].squeeze(1), starts(th, 4)[:, :, 3])
                v.tensor_tensor(yv[:, bass.ds(c, 1), 0:TP].squeeze(1), th[:, 0:TP], gy[:, 0:TP], ALU.mult)
                v.tensor_tensor(yv[:, bass.ds(c, 1), TP:T].squeeze(1).rearrange("p (b s) -> p b s", s=DEC_S), starts(th, 4),
                                gy[:, TP:T].rearrange("p (b s) -> p b s", s=DEC_S), ALU.mult).then_inc(y_ok, 1)

            def recurrent(i):
                ch.loop(i, 16)
                for j in range(4):
                    c = i * 2 + j // 2
                    split_lo(dve, RNN, i, j + 1)
                    if j == 2:
                        chain_rnn(i * 2)
                    if j:
                        a_out(pairs(RNN, i, j - 1))
                    if j % 2 == 0:
                        b = (RNN.g0 + j) % 2
                        dve.wait_ge(unit_done, RNN.g(i, j) + 1)
                        bias = rb[:, 0, bass.ds(c, 1)]
                        after(dve, st_conv, c)
                        v.tensor_scalar(rxp[:, 3:3 + TP], bank[b][:, 0:TP], bias, None, ALU.add)
                        v.tensor_scalar(starts(rxp, 7, TP + 3)[:, :, 3:7],
                                        bank[b][:, TP:T].rearrange("p (b s) -> p b s", s=DEC_S), bias, None,
                                        ALU.add).then_inc(acc_free[b], 1)
                        read_out(dve, RNN.g0, i, 4, j)
                        dve.wait_ge(st_pre, c + 2)
                        w = [convw[:, k, bass.ds(c, 1)] for k in range(4)]
                        ch(v.tensor_scalar(xc[:, 0:L], rxp[:, 3:3 + L], w[3], lrup[:, 0, bass.ds(c, 1)], ALU.mult, ALU.add))
                        for k in range(3):
                            ins = v.scalar_tensor_tensor(xc[:, 0:L], rxp[:, k:k + L], w[k], xc[:, 0:L], ALU.mult, ALU.add)
                            if k < 2:
                                ch(ins)
                        ins.then_inc(conv_ok, 1)
                    if j == 3:
                        a_out(pairs(RNN, i, 3))
                        chain_rnn(i * 2 + 1)
            steps(dve, RNN.n, recurrent)
            ch.end(RNN.n)

            NEGMAX = -3.0e38
            for g2 in range(2):
                with dve.Fori(0, 4) as i:
                    t = i + 4 * g2
                    ch.loop(i, 15)
                    split_lo(dve, MRG, t, 1)
                    dve.wait_ge(scored, t * 3 + 1)
                    dve.wait_ge(bz_in, t * 32 + 32)

                    def scores(out_, ps, bias, col):
                        return v.tensor_tensor_reduce(out_, ps, bias, 1.0, NEGMAX, ALU.add, ALU.max, st[:, 0, col:col + 1])

                    h0 = t * 2
                    c5 = bank[5][:, 0:4 * NCMP].rearrange("p (q h n) -> p q h n", q=2, h=2)
                    pc4 = pcs[:].rearrange("p (q h) n -> p q h n", q=2)
                    v.tensor_tensor(pc4, c5, biasC[:, :, :, bass.ds(h0, 2)].rearrange("p q n h -> p q h n"), ALU.add)
                    for c in range(4):
                        ins = scores(pb[:, 0, c * P:(c + 1) * P], bank[4][:, c * P:(c + 1) * P], bz[:, c // 2, P:TP], c)
                    ch(ins)
                    ch(v.tensor_reduce(stc[:, 0, :], pcs[:], AX.X, ALU.max))
                    v.tensor_scalar(st[:, 1, 0:4], st[:, 0, 0:4], -1.0, None, ALU.mult)
                    v.tensor_tensor(pcs[:], pcs[:], bc(stc[:, 0, :], NCMP), ALU.subtract).then_inc(s_read, 1)
                    dve.wait_ge(scored, t * 3 + 2)
                    split_lo(dve, MRG, t, 2)
                    for c in range(4):
                        ins = scores(pb[:, 1 + c // 2, (c % 2) * TP:(c % 2 + 1) * TP],
                                     bank[2 + c // 2][:, (c % 2) * TP:(c % 2 + 1) * TP], bz[:, c // 2, :], 4 + c)
                    m1 = ch.mark(ins)
                    dve.wait_ge(scored, t * 3 + 3)
                    ch.wait(m1)
                    v.tensor_scalar(st[:, 1, 4:8], st[:, 0, 4:8], -1.0, None, ALU.mult).then_inc(s_read, 1)
                    for br in range(2):
                        scores(pss[:, br, :], bank[6 + br][:, 0:PAST + DEC_S], biasS[:], 8 + br)
                    ch(scores(pcc[:], bank[6][:, 264:264 + NCMP], biasCS[:], 10))
                    v.tensor_scalar(st[:, 1, 8:11], st[:, 0, 8:11], -1.0, None, ALU.mult).then_inc(s_read, 1)

                    gt = gtok[:, :, bass.ds(t * 6, 6)].rearrange("p q (h b) -> p q h b", b=3)
                    dve.wait_ge(exped, t * 3 + 1)
                    ch(v.reciprocal(st[:, 3, 0:4], st[:, 2, 0:4]))
                    ch(v.tensor_tensor(pc4, pc4, maskC[:].unsqueeze(2).broadcast_to([P, 2, 2, NCMP]), ALU.mult))
                    ch(v.tensor_tensor(st[:, 3, 0:4].rearrange("p (h b) -> p h b", b=2),
                                       st[:, 3, 0:4].rearrange("p (h b) -> p h b", b=2), gt[:, 0, :, 1:3], ALU.mult))
                    p0_ = pb[:, 0, :].rearrange("p (c n) -> p c n", n=P)
                    v.tensor_tensor(p0_, p0_, bc(st[:, 3, 0:4], P), ALU.mult)
                    ch(v.tensor_reduce(stc[:, 1, :], pcs[:], AX.X, ALU.add))
                    ch(v.tensor_scalar(stc[:, 1, :], stc[:, 1, :], 1e-30, None, ALU.max))
                    ch(v.reciprocal(stc[:, 2, :], stc[:, 1, :]))
                    c2 = stc[:, 2, :].rearrange("p (q h) -> p q h", q=2)
                    ch(v.tensor_tensor(c2, c2, gt[:, :, :, 0], ALU.mult))
                    v.tensor_tensor(pcs[:], pcs[:], bc(stc[:, 2, :], NCMP), ALU.mult).then_inc(p_ok, 1)
                    split_lo(dve, MRG, t, 3)
                    dve.wait_ge(exped, t * 3 + 2)
                    ch(v.reciprocal(st[:, 3, 4:8], st[:, 2, 4:8]))
                    w1_ = st[:, 3, 4:8].rearrange("p (h b) -> p h b", b=2)
                    ch(v.tensor_tensor(w1_, w1_, gt[:, 1, :, 1:3], ALU.mult))
                    p1_ = pb[:, 1:3, :].rearrange("p h (b n) -> p (h b) n", n=TP)
                    v.tensor_tensor(p1_, p1_, bc(st[:, 3, 4:8], TP), ALU.mult).then_inc(p_ok, 1)
                    dve.wait_ge(exped, t * 3 + 3)
                    ch(v.reciprocal(st[:, 3, 8:11], st[:, 2, 8:11]))
                    gst = gs[:, bass.ds(t, 1), :].squeeze(1)
                    v.tensor_tensor(st[:, 3, 8:10], st[:, 3, 8:10], gst[:, 1:3], ALU.mult)
                    ch(v.tensor_tensor(st[:, 3, 10:11], st[:, 3, 10:11], gst[:, 0:1], ALU.mult))
                    v.tensor_tensor(pss[:], pss[:], bc(st[:, 3, 8:10], PAST + DEC_S), ALU.mult)
                    v.tensor_scalar(pcc[:], pcc[:], st[:, 3, 10:11], None, ALU.mult).then_inc(p_ok, 1)
                    split_lo(dve, MRG, t, 4)
                    dve.wait_ge(pt_mm, t * 3 + 1)
                    v.tensor_copy(pT[:, 0, :], bank[4][:])
                    v.tensor_copy(pcT[:], bank[5][0:NCMP, :]).then_inc(pt_dve, 1)
                    dve.wait_ge(pv_mm, t + 1)
                    dve.wait_ge(staged, t * 8 + 8)
                    v.tensor_copy(qT[:, bass.ds(t, 1), 0:TP].squeeze(1), bank[2][:, 0:TP]).then_inc(o_ok, 1)
                    v.tensor_copy(qT[:, :, bass.ds(t * DEC_S + TP, DEC_S)],
                                  bank[3][:, 0:32].rearrange("p (c s) -> p c s", s=DEC_S)).then_inc(o_ok, 1)
                ch.end(4)

            dve.wait_ge(osp_hi, 1)
            v.tensor_tensor(olo[:], qT[:], f32(ohi[:]), ALU.subtract).then_inc(osp_lo, 1)
            dve.wait_ge(osp_hi, 2)
            v.tensor_tensor(ylo[:], yv[:], f32(yhi[:]), ALU.subtract).then_inc(osp_lo, 1)
            with dve.Fori(0, CMB.n) as i:
                for j in range(4):
                    n = i * 4 + j
                    b = (CMB.g0 + j) % 2
                    split_lo(dve, CMB, i, j + 1)
                    if j % 2:
                        a_out(pairs(CMB, i, j // 2))
                    dve.wait_ge(unit_done, CMB.g(i, j) + 1)
                    dve.wait_ge(mgl_in[j % 2], i * 32 + 16 * (j // 2 + 1))
                    v.scalar_tensor_tensor(mt[:, 0, :], mgl[:, j % 2, 0, :], 1.0, bank[b][:, 0:T], ALU.add, ALU.mult)
                    v.scalar_tensor_tensor(mt[:, 1, :], mgl[:, j % 2, 1, :], 1.0, bank[2 + b][:, 0:T], ALU.add,
                                           ALU.mult).then_inc(acc_free[b], 1)
                    read_out(dve, CMB.g0, i, 4, j)
                    v.tensor_tensor(mt[:, 0, :], mt[:, 0, :], mt[:, 1, :], ALU.add).then_inc(m_add, 1)
                    dve.wait_ge(m_hi, n + 1)
                    v.scalar_tensor_tensor(xlo[:, bass.ds(n, 1), :].squeeze(1), mt[:, 0, :], 0.5,
                                           f32(xhi[:, bass.ds(n, 1), :].squeeze(1)), ALU.mult, ALU.subtract).then_inc(m_ok, 1)
                    dve.wait_ge(m_ok, n + 1)

            def gated(o0, i, per, j, g, keep, z0):
                b, n = (o0 + j) % 2, i * per + j
                v.tensor_scalar(zt[:, 0:TP], bank[b][:, 0:TP], ada[:, bass.ds(n + g, 1), 0:1].squeeze(1), None, ALU.mult)
                v.tensor_tensor(zt[:, TP:T].rearrange("p (b s) -> p b s", s=DEC_S),
                                bank[b][:, TP:T].rearrange("p (b s) -> p b s", s=DEC_S),
                                bc(ada[:, bass.ds(n + g, 1), 1:NSEQ].squeeze(1), DEC_S), ALU.mult).then_inc(acc_free[b], 1)
                read_out(dve, o0, i, per, j)
                zc = z[:, bass.ds(n, 1), :].squeeze(1)
                v.scalar_tensor_tensor(zc, zc, keep, zt[:], ALU.mult, ALU.add).then_inc(z_ok, 1)
                dve.wait_ge(z_ok, n + (z0 + 1))

            dve.wait_ge(z_in, 16)
            with dve.Fori(0, OUT.n) as i:
                for j in range(4):
                    split_lo(dve, OUT, i, j + 1)
                    if j % 2:
                        a_out(pairs(OUT, i, j // 2))
                    dve.wait_ge(unit_done, OUT.g(i, j) + 1)
                    gated(OUT.g0, i, 4, j, 2 * DC, ALPHA, 0)

            def norm_dve(n):
                dve.wait_ge(ln_mean, n + 1)
                ch(v.tensor_copy(mean[:], bank[2][:, 0:T]))

                def over(q):
                    return z[:, 4 * q:4 * q + 4, :]

                for q in range(4):
                    v.tensor_tensor(over(q), over(q), mean[:].unsqueeze(1).broadcast_to([P, 4, T]),
                                    ALU.subtract).then_inc(ln_c, 1)
                dve.wait_ge(ln_std, n + 1)
                ch(v.reciprocal(rstd[:], rstd[:]))
                for q in range(4):
                    v.tensor_tensor(over(q), over(q), rstd[:].unsqueeze(1).broadcast_to([P, 4, T]),
                                    ALU.mult).then_inc(ln_n, 1)

            norm_dve(0)
            dve.wait_ge(ln_out, DC)
            modulate(1, z, sq, 3 * DC, 4 * DC)
            for half in range(2):
                def fin(i, last):
                    for j in range(4):
                        split_lo(dve, FIN[half], i, j + 1, KUNIT if last and j == 3 else UNIT)
                        if j % 2:
                            c = i * 2 + (j // 2 + HALF * half)
                            b = (O_FIN[half] + j) % 2
                            dve.wait_ge(unit_done, FIN[half].g(i, j) + 1)
                            read_out(dve, O_FIN[half], i, 4, j - 1)
                            v.tensor_tensor(ht[:, j // 2], ht[:, j // 2], bank[b][:, 0:T], ALU.mult).then_inc(acc_free[b], 1)
                            read_out(dve, O_FIN[half], i, 4, j)
                            dve.wait_ge(h_hi, c + 1)
                            hc = bass.ds(i * 2 + j // 2, 1)
                            v.tensor_tensor(hlo[:, hc, :].squeeze(1), ht[:, j // 2], f32(hhi[:, hc, :].squeeze(1)),
                                            ALU.subtract).then_inc(h_lo, 1)

                def fout(i, last):
                    for j in range(4):
                        if last and j == 3:
                            if half == 0:
                                split_lo(dve, FOUT[half], i, j + 1, UNIT)
                        else:
                            split_lo(dve, FOUT[half], i, j + 1, KUNIT)
                        if j % 2:
                            dve.wait_ge(unit_done, FOUT[half].g(i, j) + 1)
                            gated(O_FOUT[half], i, 2, j // 2, 5 * DC, ALPHA if half == 0 else 1.0, DC * (1 + half))

                with dve.Fori(0, FIN[half].n - 1) as i:
                    fin(i, False)
                fin(FIN[half].n - 1, True)
                with dve.Fori(0, FOUT[half].n - 1) as i:
                    fout(i, False)
                fout(FOUT[half].n - 1, True)
            norm_dve(1)


def lay_out(x_prompt, x_sample, c_prompt, c_sample, cache_cmp_kv, cache_slc_kv, cache_win_kv, state_conv, state_rnn_h,
            page_table, rel_bias, w_ada, b_ada, w_in, b_in, cmp_pos, cmp_w1, cmp_w2, w_attn_o, conv_w, conv_b, lru_wa,
            lru_ba, lru_wi, lru_bi, lru_lambda, w_rnn_o, w_out, w_ffn_in, w_ffn_out, ln_g, ln_b):
    import numpy as np

    heads = np.array([[j % 4 + 8 * (j // 4), j % 4 + 8 * (j // 4) + 4] for j in range(NP_)])
    hcols = (heads.reshape(-1)[:, None] * HD + np.arange(HD)).reshape(-1)

    def blocks(w, kc=None):
        k, n = w.shape
        return w.reshape(k // P, P, n // P, P).transpose(2, 1, 0, 3).reshape(n // P, P, -1)

    def cols(v_):
        return np.ascontiguousarray(v_.reshape(-1, P).T)

    w, b = w_in[0], b_in[0]
    cuts = np.cumsum([H * HD, 512, 512, 512, 3 * H, DR, DR, 2 * D])
    wq, wkv, wg = w[:, :cuts[0]], w[:, cuts[0]:cuts[3]], w[:, cuts[3]:cuts[4]]
    wrx, wry, wm = w[:, cuts[4]:cuts[5]], w[:, cuts[5]:cuts[6]], w[:, cuts[6]:]
    gcols = (heads.reshape(-1)[:, None] * 3 + np.arange(3)).reshape(-1)
    wa = blocks(w_ada[0])
    wr = np.stack([blocks(wrx), blocks(wry)], 1).reshape(2 * RC, P, -1)
    ao, ro = blocks(w_attn_o[0][hcols]), blocks(w_rnn_o[0])
    comb = np.concatenate([ao, ro], 2)
    wo = blocks(w_out[0])
    fi = w_ffn_in[0]
    ff = np.stack([blocks(fi[:, :FF]), blocks(fi[:, FF:])], 1).reshape(2 * FC, P, -1)

    def woven(st_, g, a_):
        out_, gi, ai = [], 0, st_.a0
        for _ in range(st_.n):
            for p in range(st_.U):
                if p in st_.G:
                    out_.append(g[gi])
                    gi += 1
                else:
                    out_.append(a_[ai])
                    ai += 1
        return out_

    units = np.stack(woven(INIT, [], wa) + list(blocks(wq[:, hcols])) + list(blocks(wkv)) + woven(RNN, wr, wa)
                     + list(blocks(wm)) + woven(CMB, comb, wa) + woven(OUT, wo, wa) + list(ff))
    fo = w_ffn_out[0].reshape(2, 2, KS, P, DC, P).transpose(0, 4, 1, 3, 2, 5).reshape(4 * DC, P, KUNIT)

    x = np.concatenate([x_prompt.reshape(TP, D), x_sample.reshape(TS, D)], 0)
    c = np.concatenate([c_prompt, c_sample], 0)

    def feat(m):
        return np.ascontiguousarray(m.reshape(m.shape[0], -1, P).transpose(2, 1, 0))

    def keys(k_):
        n, t = k_.shape[:2]
        return np.ascontiguousarray(k_.reshape(n, t, 2, 2, HD).transpose(0, 3, 4, 2, 1).reshape(n, P, 2, t))

    slc, cmp_, win = cache_slc_kv[0], cache_cmp_kv[0], cache_win_kv[0]
    n_phys = slc.shape[0]

    dist = np.arange(0, 512)
    exact = 16
    ratio = np.log(np.maximum(dist, 1).astype(np.float32) / np.float32(exact)) / np.float32(np.log(128 / exact))
    bucket = np.where(dist < exact, dist, np.minimum(exact + (ratio * np.float32(32 - exact)).astype(np.int32), 31))

    def one_hot(dists):
        m = np.zeros((33, len(dists)), np.float32)
        for n, d in enumerate(dists):
            if d >= 0:
                m[bucket[d], n] = 1.0
            else:
                m[32, n] = NEG
        return m

    mask = np.zeros((P, 2, NCMP), np.float32)
    for qt in range(2):
        for n in range(NCMP):
            mask[:, qt, n] = (np.arange(P) + qt * P - (STRIDE * n + CMP - 1)) >= 0
    selq = np.zeros((P, NSEQ), np.float32)
    for q in range(4):
        selq[32 * q + np.arange(NSEQ), np.arange(NSEQ)] = 1.0
    pos = cmp_pos[0].transpose(0, 2, 1)
    w1 = cmp_w1[0].transpose(0, 2, 1, 3)
    ins = {
        "w_units": units, "w_ffn_out_units": fo, "x": feat(x), "cond": feat(c),
        "b_ada": cols(b_ada[0]), "lnp": np.stack([np.stack([cols(ln_g[0][n]), cols(ln_b[0][n])], 1) for n in range(2)], 1),
        "ident": np.eye(P, dtype=np.float32), "selq": selq, "oh": one_hot(np.arange(512) - 255),
        "ohr": one_hot(259 - np.arange(392)), "rel": rel_bias[:, heads.reshape(-1)], "mask_c": mask,
        "w_gate": wg[:, gcols].reshape(DC, P, 48).transpose(1, 0, 2), "b_q": cols(b[:cuts[0]][hcols]),
        "b_kv": cols(b[cuts[0]:cuts[3]]).reshape(P, 3, 4), "b_gate": b[cuts[3]:cuts[4]][gcols].reshape(48, 1),
        "b_r": cols(b[cuts[4]:cuts[6]]).reshape(P, 2, RC), "conv_w": np.stack([cols(conv_w[0][k]) for k in range(4)], 1),
        "lru_p": np.stack([cols(m[0]) for m in (conv_b, lru_ba, lru_bi, lru_lambda)], 1),
        "conv_state": state_conv[0].reshape(DEC_B, 3, RC, P).transpose(3, 2, 0, 1), "rnn_h": feat(state_rnn_h[0]),
        "b_merge": cols(b[cuts[6]:]), "page_table": page_table.reshape(1, -1),
        "cmp_w1": np.concatenate([w1, w1], 1), "cmp_w2": cmp_w2[0], "cmp_pos": np.concatenate([pos, pos], 1),
        "lru_wa": lru_wa[0], "lru_wi": lru_wi[0],
        "cmp_k": keys(cmp_[:, :, 0]), "cmp_v": keys(cmp_[:, :, 1]), "slc_k": keys(slc[:, :, 0]),
        "slc_v": slc[:, :, 1].reshape(n_phys, PAGE, 256), "win_k": keys(win[:, :, 0]),
        "win_v": win[:, :, 1].reshape(DEC_B, 2, P, 256).transpose(0, 2, 1, 3),
    }
    return {k_: np.ascontiguousarray(v_) for k_, v_ in ins.items()}, n_phys


_OUTS = {"y": [P, DC, T], "kv": [P, 3, 4, T], "conv": [P, RC, NSEQ, 3], "h": [P, RC, NSEQ]}


def kernel(**inputs):
    import numpy as np
    import concourse.bacc as bacc
    from concourse.bass_utils import run_bass_kernel_spmd

    ins, n_phys = lay_out(**{k: np.asarray(v) for k, v in inputs.items()})
    nc = bacc.Bacc("TRN2", target_bir_lowering=False, num_devices=1)
    arrays = {f"in_{k}": v for k, v in ins.items()}
    a = {k: nc.dram_tensor(f"in_{k}", list(v.shape), mybir.dt.from_np(v.dtype), kind="ExternalInput").ap()
         for k, v in ins.items()}
    a["n_phys"] = n_phys
    out = {k: nc.dram_tensor(f"out_{k}", s, F32, kind="ExternalOutput").ap() for k, s in _OUTS.items()}
    build(nc, a, out)
    r = run_bass_kernel_spmd(nc, [arrays], core_ids=[0]).results[0]
    y = r["out_y"].transpose(2, 1, 0).reshape(T, D)
    kv = r["out_kv"].reshape(2, HD, 3, 2, 2, T).transpose(2, 5, 3, 4, 0, 1).reshape(3, T, 2, KVH, HD)
    conv = r["out_conv"].transpose(2, 3, 1, 0).reshape(NSEQ, 3, DR)
    h = r["out_h"].transpose(2, 1, 0).reshape(NSEQ, DR)
    c_ = np.ascontiguousarray
    kvp = [c_(kv[k, :TP])[None, None] for k in range(3)]
    kvs = [c_(kv[k, TP:].reshape(DEC_B, DEC_S, 2, KVH, HD))[None] for k in range(3)]
    return (c_(y[:TP])[None], c_(y[TP:]).reshape(DEC_B, DEC_S, D), kvp[0], kvp[1], kvp[2], c_(conv[:1])[None], c_(h[:1])[None],
            kvs[0], kvs[1], kvs[2], c_(conv[1:])[None], c_(h[1:])[None])
```

```python
from contextlib import ExitStack

import concourse.bass as bass
from concourse import mybir

F32 = mybir.dt.float32
F32R = mybir.dt.float32r
I32 = mybir.dt.int32
ACT = mybir.ActivationFunctionType
ALU = mybir.AluOpType
AX = mybir.AxisListType

P = 128
D = 2048
DC = D // P
TP, DEC_B, DEC_S = 256, 8, 4
TS = DEC_B * DEC_S
T = TP + TS
NSEQ = 1 + DEC_B
H, KVH, HD = 16, 4, 64
NP_ = 8
PAST, PAGE = 256, 128
STRIDE, CMP = 16, 32
NCMP = PAST // STRIDE - 1
DR = 1024
RC = DR // P
FF = 5632
FC = FF // P
HALF = FC // 2
KS = HALF // 2
ALPHA = 2.0 ** 0.25
LRU_C = 8.0
SCALE = HD ** -0.5
EPS = 1e-5
NEG = -1e30
UNIT = DC * P
KUNIT = KS * P
RAW_SLOTS = 4
LPAD = 3 + TP + 7 * DEC_B
L = LPAD - 3
S0 = TP + 3
RV = 512
BZ = 384
NADA = 6 * DC


class Stage:

    def __init__(self, pattern, n, r0, g0, a0=0, lead=0):
        self.lead = lead
        self.n, self.r0, self.g0, self.a0, self.U = n, r0, g0, a0, len(pattern)
        self.G = [p for p, c in enumerate(pattern) if c == "G"]
        self.A = [p for p, c in enumerate(pattern) if c == "A"]
        assert (r0 % RAW_SLOTS == 0 or not self.G) and self.U % RAW_SLOTS == 0 and len(self.G) % 2 == 0 and lead % RAW_SLOTS == 0
        self.r_end, self.g_end, self.a_end = r0 + n * self.U, g0 + n * len(self.G), a0 + n * len(self.A)

    def raw(self, i, pos):
        k = i * (self.U // RAW_SLOTS) + (self.r0 + pos) // RAW_SLOTS
        if isinstance(i, int) and i == 0 and pos == 0:
            k -= self.lead // RAW_SLOTS
        return (self.r0 + pos) % RAW_SLOTS, k

    def rawG(self, i, j):
        n = len(self.G)
        return self.raw(i, self.U * (j // n) + self.G[j % n])

    def g(self, i, j):
        return i * len(self.G) + (self.g0 + j)


INIT = Stage("AAAAAAAA", 4, 0, 0, 0)
QS = Stage("GGGGAAGGAAGG", 1, INIT.r_end, 1, INIT.a_end)
KVS = Stage("GAAGGAAG", 3, QS.r_end, QS.g_end, QS.a_end)
RNN = Stage("GAAGGAAG", 4, KVS.r_end, KVS.g_end, KVS.a_end)
MID = Stage("AAAA", 1, RNN.r_end + 1, 0, RNN.a_end)
MRG = Stage("GGGG", 8, RNN.r_end + MID.U, RNN.g_end, lead=MID.U)
CMB = Stage("GAAGGAAG", 4, MRG.r_end, MRG.g_end, MID.a_end)
OUT = Stage("GGGG", 4, CMB.r_end, CMB.g_end)
LNA = Stage("A" * 12, 1, OUT.r_end + 1, 0, CMB.a_end)
FIN = [None, None]
FOUT = [None, None]
FIN[0] = Stage("GGGG", 11, OUT.r_end + LNA.U, OUT.g_end, lead=LNA.U)
FOUT[0] = Stage("GGGG", 8, FIN[0].r_end, FIN[0].g_end)
FIN[1] = Stage("GGGG", 11, FOUT[0].r_end, FOUT[0].g_end)
FOUT[1] = Stage("GGGG", 8, FIN[1].r_end, FIN[1].g_end)
assert LNA.a_end == NADA
O_FIN = [FIN[0].g0, FIN[0].g_end + 16]
O_FOUT = [FIN[0].g_end, FIN[0].g_end + 16 + 2 * HALF]


class Chain:

    def __init__(self, eng, sem):
        self.eng, self.sem, self.n, self.i, self.per = eng, sem, 0, None, 0

    def loop(self, i, per):
        self.i, self.per, self.k = i, per, 0

    def end(self, times):
        assert self.k == self.per, f"{self.k} steps, {self.per} said"
        self.n, self.i = self.n + self.per * times, None

    def mark(self, ins):
        ins.then_inc(self.sem, 1)
        if self.i is None:
            self.n += 1
            return self.n
        self.k += 1
        return self.i * self.per + (self.n + self.k)

    def wait(self, value):
        self.eng.wait_ge(self.sem, value)

    def __call__(self, ins):
        self.wait(self.mark(ins))


def build(nc, a, out):
    with ExitStack() as ctx:
        def sem(name):
            return ctx.enter_context(nc.semaphore(name))

        def sbuf(stack, name, shape, dt=F32):
            return stack.enter_context(nc.sbuf_tensor(name, shape, dt))

        def dram(name, shape):
            return nc.dram_tensor(name, shape, F32).ap()

        toep = dram("toep", [H * P * RV])
        mgate = dram("mgate", [2 * DC, P, T])
        gscr = dram("gscr", [6, NP_, DEC_S, DEC_B])

        raw = sbuf(ctx, "raw", [P, RAW_SLOTS, UNIT])
        whi = [sbuf(ctx, f"whi{e}", [P, UNIT], F32R) for e in range(2)]
        wlo = [sbuf(ctx, f"wlo{e}", [P, UNIT], F32R) for e in range(2)]
        xhi = sbuf(ctx, "xhi", [P, DC, T], F32R)
        xlo = sbuf(ctx, "xlo", [P, DC, T], F32R)
        ada = sbuf(ctx, "ada", [P, NADA, NSEQ])
        bada = sbuf(ctx, "bada", [P, NADA])
        condp = sbuf(ctx, "condp", [P, DC, 32])
        adp = sbuf(ctx, "adp", [P, 4, P])
        selq = sbuf(ctx, "selq", [P, NSEQ])
        lnp = sbuf(ctx, "lnp", [P, 2, 2, DC])
        ones = sbuf(ctx, "ones", [P, P])
        epst = sbuf(ctx, "epst", [P, 1])
        ident = sbuf(ctx, "ident", [P, P])
        bank = [ctx.enter_context(nc.psum_tensor(f"bank{b}", [P, 512], F32)) for b in range(8)]

        pz = ExitStack()
        ohr = sbuf(pz, "ohr", [33, 4 + RV])
        rel1 = sbuf(pz, "rel1", [33, H])
        selt = sbuf(pz, "selt", [33, DEC_S, P])
        pz.close()
        s1 = ExitStack()
        qT = sbuf(s1, "qT", [P, NP_, T])
        kvT = sbuf(s1, "kvT", [P, 3, 4, T])
        kcT = sbuf(s1, "kcT", [P, 2, NSEQ, NCMP])
        hv = sbuf(s1, "hv", [P, 2, NSEQ, NCMP])
        vtok = sbuf(s1, "vtok", [P, 2, 512])
        vcp = sbuf(s1, "vcp", [NCMP, 256])
        gtok = sbuf(s1, "gtok", [P, 2, 6 * NP_])
        gs = sbuf(s1, "gs", [P, DEC_B, 3])
        w2b = sbuf(s1, "w2b", [P, 2, P])
        biasS = sbuf(s1, "biasS", [P, PAST + DEC_S])
        biasCS = sbuf(s1, "biasCS", [P, NCMP])
        maskC = sbuf(s1, "maskC", [P, 2, NCMP])
        yv = sbuf(s1, "yv", [P, RC, T])
        btanh = sbuf(s1, "btanh", [P, 2 * DC])
        cstash = sbuf(s1, "cstash", [P, RC, NSEQ, 3])
        hstash = sbuf(s1, "hstash", [P, RC, NSEQ])
        ptab = sbuf(s1, "ptab", [1, 2 * DEC_B], I32)
        bz = sbuf(s1, "bz", [P, 2, BZ])
        qz = sbuf(s1, "qz", [P, 2, TP])
        qzs = sbuf(s1, "qzs", [P, KVH, 32])
        p0 = ExitStack()
        xt = sbuf(p0, "xt", [P, DC, T])
        xm = sbuf(p0, "xm", [P, 2, 2, T])
        graw = sbuf(p0, "graw", [P, DC, 6 * NP_])
        cond = sbuf(p0, "cond", [P, DC, NSEQ])
        p0.close()
        p1 = ExitStack()
        rrow = sbuf(p1, "rrow", [H, RV])
        cmp_rows = sbuf(p1, "cmp_rows", [P, 2 * NSEQ + 1, PAST])
        rxp = sbuf(p1, "rxp", [P, LPAD])
        gy = sbuf(p1, "gy", [P, T])
        xc = sbuf(p1, "xc", [P, LPAD])
        rg = sbuf(p1, "rg", [P, LPAD])
        ig = sbuf(p1, "ig", [P, LPAD])
        th = sbuf(p1, "th", [P, LPAD])
        av = sbuf(p1, "av", [P, LPAD])
        hk = sbuf(p1, "hk", [P, 2 * NSEQ * NCMP])
        w1d = sbuf(p1, "w1d", [P, CMP, HD])
        gT = sbuf(p1, "gT", [6 * NP_, T])
        gTs = sbuf(p1, "gTs", [6 * NP_, TS])
        qb = sbuf(p1, "qb", [P, NP_])
        kvb = sbuf(p1, "kvb", [P, 3, 4])
        gb = sbuf(p1, "gb", [6 * NP_, 1])
        rb = sbuf(p1, "rb", [P, 2, RC])
        wad = sbuf(p1, "wad", [P, 2, RC, P])
        convw = sbuf(p1, "convw", [P, 4, RC])
        lrup = sbuf(p1, "lrup", [P, 4, RC])
        sp = sbuf(p1, "sp", [P, 6, RC])
        cst = sbuf(p1, "cst", [P, RC, DEC_B, 3])
        h0t = sbuf(p1, "h0t", [P, RC, DEC_B])
        ah = sbuf(p1, "ah", [P, DEC_B])
        wcur = sbuf(p1, "wcur", [P, 2, P])
        cbias = sbuf(p1, "cbias", [P, 1])
        p1.close()
        p2 = ExitStack()
        ks = sbuf(p2, "ks", [P, 2, 2, PAST + DEC_S])
        vs = sbuf(p2, "vs", [P, 2, 2, 256])
        vn = sbuf(p2, "vn", [P, 2, 2, DEC_S])
        vnew = sbuf(p2, "vnew", [DEC_S, 512])
        kcs = sbuf(p2, "kcs", [P, 2, NCMP])
        hvs = sbuf(p2, "hvs", [P, 2, NCMP])
        vcs = sbuf(p2, "vcs", [NCMP, 256])
        pb = sbuf(p2, "pb", [P, 3, 512])
        pcs = sbuf(p2, "pcs", [P, 4, NCMP])
        pss = sbuf(p2, "pss", [P, 2, PAST + DEC_S])
        pcc = sbuf(p2, "pcc", [P, NCMP])
        pT = sbuf(p2, "pT", [P, 3, 512])
        pcT = sbuf(p2, "pcT", [NCMP, 512])
        psT = sbuf(p2, "psT", [P, 512])
        psn = sbuf(p2, "psn", [DEC_S, 256])
        psc = sbuf(p2, "psc", [NCMP, P])
        st = sbuf(p2, "st", [P, 4, 12])
        stc = sbuf(p2, "stc", [P, 3, 4])
        mg = sbuf(p2, "mg", [P, 2, T])
        p2.close()
        p3 = ExitStack()
        ohi = sbuf(p3, "ohi", [P, NP_, T], F32R)
        olo = sbuf(p3, "olo", [P, NP_, T], F32R)
        yhi = sbuf(p3, "yhi", [P, RC, T], F32R)
        ylo = sbuf(p3, "ylo", [P, RC, T], F32R)
        mgl = sbuf(p3, "mgl", [P, 2, 2, T])
        mt = sbuf(p3, "mt", [P, 2, T])
        p3.close()
        s1.close()
        s2 = ExitStack()
        z = sbuf(s2, "z", [P, DC, T])
        hhi = sbuf(s2, "hhi", [P, HALF, T], F32R)
        hlo = sbuf(s2, "hlo", [P, HALF, T], F32R)
        ht = sbuf(s2, "ht", [P, 2, T])
        zt = sbuf(s2, "zt", [P, T])
        mean = sbuf(s2, "mean", [P, T])
        rstd = sbuf(s2, "rstd", [P, T])
        zsum = sbuf(s2, "zsum", [P, T])
        sq = sbuf(s2, "sq", [P, 2, 2, T])
        s2.close()

        raw_in = [sem(f"raw_in{s}") for s in range(RAW_SLOTS)]
        raw_used = [sem(f"raw_used{s}") for s in range(RAW_SLOTS)]
        hi_done = sem("hi_done")
        glo_done = sem("glo_done")
        unit_done = sem("unit_done")
        acc_free = [sem("acc_free0"), sem("acc_free1")]
        ada_cp = sem("ada_cp")
        ada_t = sem("ada_t")
        ada_out = sem("ada_out")
        c_in, x_in, w_in_s, z_in = sem("c_in"), sem("x_in"), sem("w_in_s"), sem("z_in")
        a_in, b_in = sem("a_in"), sem("b_in")
        pool_set, dve_set, act_set = sem("pool_set"), sem("dve_set"), sem("act_set")
        cond_ok, bias_mm, bias_ok = sem("cond_ok"), sem("bias_mm"), sem("bias_ok")
        toep_out = sem("toep_out")
        mod_f, mod_hi, mod_lo, mod_lo2 = sem("mod_f"), sem("mod_hi"), sem("mod_lo"), sem("mod_lo2")
        gate_t, gt_ok = sem("gate_t"), sem("gt_ok")
        g_out, g_in = sem("g_out"), sem("g_in")
        vt_mm, vt_ok = sem("vt_mm"), sem("vt_ok")
        rows_in, rows_cp, w1_in, cmp_mm, cmp_act = sem("rows_in"), sem("rows_cp"), [sem("w1k_in"), sem("w1v_in")], sem("cmp_mm"), sem("cmp_act")
        w2_mm, kc_ok = sem("w2_mm"), sem("kc_ok")
        st_pre, st_conv = sem("st_pre"), sem("st_conv")
        conv_ok, rgate_mm, rg_act, q_ok, sq_ok, y_ok = (sem(n) for n in (
            "conv_ok", "rgate_mm", "rg_act", "q_ok", "sq_ok", "y_ok"))
        gy_ok, wc_ok = sem("gy_ok"), sem("wc_ok")
        bz_in, k_in, v_in, staged, scored, extra_mm, extra_ok = (sem(n) for n in (
            "bz_in", "k_in", "v_in", "staged", "scored", "extra_mm", "extra_ok"))
        s_read, exped, p_ok, pt_mm, pt_act, pt_dve, pv_mm, o_ok = (sem(n) for n in (
            "s_read", "exped", "p_ok", "pt_mm", "pt_act", "pt_dve", "pv_mm", "o_ok"))
        mg_out, mgl_in = [sem("mg_out0"), sem("mg_out1")], [sem("mgl_in0"), sem("mgl_in1")]
        osp_hi, osp_lo, m_add, m_hi, m_ok = sem("osp_hi"), sem("osp_lo"), sem("m_add"), sem("m_hi"), sem("m_ok")
        z_ok, zs_add, ln_mean, ln_c, ln_sq, ln_var, ln_std, ln_n, ln_out = (sem(n) for n in (
            "z_ok", "zs_add", "ln_mean", "ln_c", "ln_sq", "ln_var", "ln_std", "ln_n", "ln_out"))
        h_hi, h_lo = sem("h_hi"), sem("h_lo")
        ln_last = sem("ln_last")
        stored, y_out = sem("stored"), sem("y_out")
        dve_c, pool_c, act_c, cb_ok = sem("dve_c"), sem("pool_c"), sem("act_c"), sem("cb_ok")

        def f32(ap):
            return ap.bitcast(F32)

        def split_hi(act, st_, i, j, size=UNIT):
            s, k = st_.rawG(i, j)
            e = (st_.g0 + j) % 2
            act.wait_ge(raw_in[s], k * 16 + 16)
            act.wait_ge(unit_done, st_.g(i, j) - 1)
            nc.scalar.copy(whi[e][:, 0:size], raw[:, s, 0:size]).then_inc(hi_done, 1)

        def split_lo(dve, st_, i, j, size=UNIT):
            s, k = st_.rawG(i, j)
            e = (st_.g0 + j) % 2
            dve.wait_ge(hi_done, st_.g(i, j) + 1)
            nc.vector.tensor_tensor(wlo[e][:, 0:size], raw[:, s, 0:size], f32(whi[e][:, 0:size]),
                                    ALU.subtract).then_inc(raw_used[s], 1)

        def after(eng, s_, value):
            if not (isinstance(value, int) and value < 1):
                eng.wait_ge(s_, value)

        def steps(eng, n, body):
            body(0)
            with eng.Fori(1, n) as i:
                body(i)

        def read_out(eng, o0, i, per, j):
            eng.wait_ge(acc_free[(o0 + j) % 2], i * (per // 2) + ((o0 + j) // 2 + 1))

        def kv_written(eng):
            read_out(eng, KVS.g0, KVS.n - 1, 4, 3)


        def bc(ap, n):
            ap = ap.unsqueeze(len(ap.shape))
            return ap.broadcast_to(list(ap.shape[:-1]) + [n])

        def starts(t, n, first=S0):
            return t[:, first:first + 7 * DEC_B].rearrange("p (b s) -> p b s", s=7)[:, :, 0:n]

        def grp(t, c0, n):
            return t[:, c0:c0 + n, TP:T].rearrange("p c (b s) -> p c b s", s=DEC_S)

        block = ctx.enter_context(nc.Block())
        N_SMALL = 16
        SMALL = 16 * N_SMALL
        N_POOL = 10

        @block.sync
        def _(sp):
            def load(st_, i, pos, first=False):
                s, k = st_.raw(i, pos)
                if not first:
                    sp.wait_ge(raw_used[s], k)
                if st_ in FOUT:
                    r = i * st_.U + (pos + st_.n * st_.U * FOUT.index(st_))
                    sp.dma_start(raw[:, s, 0:KUNIT], a["w_ffn_out_units"][r]).then_inc(raw_in[s], 16)
                else:
                    r0 = st_.r0 - (FOUT[0].n * FOUT[0].U if st_ is FIN[1] else 0)
                    r = i * st_.U + (r0 + pos)
                    if isinstance(i, int) and i == 0 and pos == 0:
                        r -= st_.lead
                    sp.dma_start(raw[:, s], a["w_units"][r]).then_inc(raw_in[s], 16)

            sp.dma_start(cond[:], a["cond"]).then_inc(c_in, 16)
            for pos in range(INIT.U):
                load(INIT, 0, pos, first=pos < RAW_SLOTS)
            with sp.Fori(1, INIT.n) as i:
                for pos in range(INIT.U):
                    load(INIT, i, pos)
            for st_ in (QS, KVS, RNN, MRG, CMB, OUT, FIN[0], FOUT[0], FIN[1], FOUT[1]):
                if st_.lead:
                    load(st_, 0, 0)
                    for pos in range(st_.lead):
                        load(MID if st_ is MRG else LNA, 0, pos)
                    for pos in range(1, st_.U):
                        load(st_, 0, pos)
                with sp.Fori(1 if st_.lead else 0, st_.n) as i:
                    for pos in range(st_.U):
                        load(st_, i, pos)
            for q in range(4):
                if q < 3:
                    sp.wait_ge(ln_out, 16 + 4 * q + 4)
                else:
                    sp.wait_ge(ln_last, 4)
                sp.dma_start(out["y"][:, 4 * q:4 * q + 4, :], z[:, 4 * q:4 * q + 4, :]).then_inc(y_out, 16)
            sp.wait_ge(y_out, 16 * 4)
            sp.wait_ge(stored, 16 * 3)

        @block.gpsimd
        def _(pool):
            def one(ins, s_, value):
                ins.then_inc(s_, 1)
                pool.wait_ge(s_, value)

            for n, (dst, v) in enumerate(((condp, 0.0), (f32(whi[0][:]), 0.0), (f32(wlo[0][:]), 0.0), (selt, 0.0), (rel1[32:33, :], 1.0),
                           (w2b, 0.0), (wad, 0.0), (ones, 1.0 / D), (epst, EPS), (gs, 0.0))):
                one(pool.memset(dst if isinstance(dst, bass.AP) else dst[:], v), pool_set, n + 1)
            pool.wait_ge(bias_ok, 1)
            pool.wait_ge(mod_lo, 8)
            for h in range(2):
                half = slice(64 * h, 64 * h + 64)
                pool.dma_start(w2b[half, :, half], a["cmp_w2"].rearrange("k d e -> d k e")).then_inc(w_in_s, 16)
                for w, name in enumerate(("lru_wa", "lru_wi")):
                    pool.dma_start(wad[half, w, :, half],
                                   a[name].rearrange("(c a) d e -> a d c e", a=2)[h]).then_inc(w_in_s, 16)
            one(pool.memset(rxp[:, 0:3], 0.0), st_pre, 1)
            one(pool.memset(cmp_rows[:, 2 * NSEQ, CMP:PAST], 0.0), rows_cp, 1)

            seqs = cmp_rows[:, 0:2 * NSEQ].rearrange("p (g s) t -> p g s t", s=NSEQ)

            def load_pages(kv, b):
                for pg in range(2):
                    page = pool.value_load(ptab[0:1, bass.ds(b * 2 + pg, 1)], min_val=0, max_val=a["n_phys"] - 1)
                    pool.dma_start(seqs[:, :, bass.ds(b, 1), pg * PAGE:(pg + 1) * PAGE],
                                   a["cmp_k" if kv == 0 else "cmp_v"][page].unsqueeze(2)).then_inc(rows_in, 16)

            def load_rest(kv):
                pool.dma_start(cmp_rows[:, 2 * NSEQ, 0:CMP], a["cmp_pos"][kv]).then_inc(rows_in, 16)
                kv_written(pool)
                one(pool.tensor_copy(seqs[:, :, DEC_B, :], kvT[:, 0, 2 * kv:2 * kv + 2, 0:TP]), rows_cp, 2 + kv)

            pool.wait_ge(b_in, SMALL)
            pool.wait_ge(unit_done, QS.g0 + 2)
            pool.dma_start(w1d[:], a["cmp_w1"][0]).then_inc(w1_in[0], 16)
            with pool.Fori(0, DEC_B) as b:
                load_pages(0, b)
            read_out(pool, 0, 0, 2, 0)
            pool.tensor_copy(gTs[:].rearrange("c (s b) -> c s b", s=DEC_S),
                             gT[:, TP:T].rearrange("c (b s) -> c s b", s=DEC_S)).then_inc(pool_c, 1)
            pool.wait_ge(pool_c, 1)
            with nc.allow_non_contiguous_dma(reason="1536 gates, once"):
                for m in range(6):
                    pool.dma_start(gscr[m].rearrange("c s b -> c (s b)"), gTs[m:48:6, :]).then_inc(g_out, 16)
                pool.wait_ge(g_out, 16 * 6)
                for g in range(KVH):
                    for k in range(3):
                        rows = gscr[(g % 2) * 3 + k, 4 * (g // 2):4 * (g // 2) + 4].rearrange("r s b -> (r s) b")
                        pool.dma_start(gs[32 * g:32 * g + 16, :, k], rows).then_inc(g_in, 16)
            for q in range(4):
                pool.wait_ge(unit_done, QS.g0 + 5 + 2 * q)
                heads = slice(H // 4 * q, H // 4 * (q + 1))
                pool.dma_start(toep.rearrange("(h p y) -> h p y", h=H, p=P)[heads],
                               rrow[heads, :].unsqueeze(1).broadcast_to([H // 4, P, RV])).then_inc(toep_out, 16)
            load_rest(0)
            def conv_states(i, loads):
                for cc in range(2):
                    c = i * 2 + cc
                    after(pool, rgate_mm, c)
                    one(pool.tensor_copy(wcur[:], wad[:, :, bass.ds(c, 1), :].squeeze(2)), wc_ok, c + 1)
                    after(pool, conv_ok, c)
                    after(pool, st_conv, c)
                    one(pool.tensor_copy(starts(rxp, 3, TP + 3), cst[:, bass.ds(c, 1)].squeeze(1)), st_pre, c + 2)
                    read_out(pool, RNN.g0, i, 4, 2 * cc)
                    one(pool.tensor_copy(cstash[:, bass.ds(c, 1), 0, :].squeeze(1), rxp[:, TP:TP + 3]), pool_c, c + 2)
                    one(pool.tensor_copy(cstash[:, bass.ds(c, 1), 1:NSEQ, :].squeeze(1),
                                         starts(rxp, 7, TP + 3)[:, :, 4:7]), st_conv, c + 1)
                    if loads:
                        if c == 0:
                            pool.wait_ge(cmp_mm, 1)
                            pool.dma_start(w1d[:], a["cmp_w1"][1]).then_inc(w1_in[1], 16)
                            load_rest(1)
                        load_pages(1, 2 * c)
                        load_pages(1, 2 * c + 1)

            pool.wait_ge(w_in_s, 16 * 6)
            conv_states(0, True)
            conv_states(1, True)
            with pool.Fori(2, RNN.n) as i:
                conv_states(i, False)
            def load_bias(t):
                for h in range(2):
                    src = toep[bass.ds((t * 2 + h) * (P * RV) + (P - 1), P * (RV - 1))].rearrange("(p y) -> p y", y=RV - 1)
                    pool.dma_start(bz[:, h], src[:, 0:BZ]).then_inc(bz_in, 16)

            one(pool.memset(qz[:], 0.0), st_pre, 10)
            one(pool.memset(qzs[:], 0.0), st_pre, 11)
            pool.wait_ge(toep_out, 64)
            load_bias(0)
            pool.wait_ge(w2_mm, 2)
            pool.wait_ge(kc_ok, 3)
            pool.wait_ge(y_ok, 8)
            pool.wait_ge(g_in, 16 * 12)

            def load_keys(t):
                for pg in range(2):
                    page = pool.value_load(ptab[0:1, bass.ds(t * 2 + pg, 1)], min_val=0, max_val=a["n_phys"] - 1)
                    pool.dma_start(ks[:, 0, :, pg * PAGE:(pg + 1) * PAGE], a["slc_k"][page]).then_inc(k_in, 16)
                pool.dma_start(ks[:, 1, :, 0:PAST], a["win_k"][t]).then_inc(k_in, 16)

            def load_values(t):
                pool.dma_start(vs[:, 1, :, :], a["win_v"][t]).then_inc(v_in, 16)
                for pg in range(2):
                    page = pool.value_load(ptab[0:1, bass.ds(t * 2 + pg, 1)], min_val=0, max_val=a["n_phys"] - 1)
                    pool.dma_start(vs[:, 0, pg, :], a["slc_v"][page]).then_inc(v_in, 16)

            def stage(t):
                for h in range(2):
                    half = slice(64 * h, 64 * h + 64)
                    one(pool.tensor_copy(qz[half, h, :], qT[half, bass.ds(t, 1), 0:TP].squeeze(1)), staged, t * 8 + (2 * h + 1))
                    one(pool.tensor_copy(qzs[half, h:KVH:2, 0:16].rearrange("p g (r s) -> p g r s", s=DEC_S),
                                         qT[half, :, bass.ds(t * DEC_S + TP, DEC_S)].rearrange("p (g r) s -> p g r s", r=4)),
                        staged, t * 8 + (2 * h + 2))
                one(pool.tensor_copy(ks[:, :, :, PAST:PAST + DEC_S], kvT[:, 1:3, 0:2, bass.ds(t * DEC_S + TP, DEC_S)]),
                    staged, t * 8 + 5)
                one(pool.tensor_copy(vn[:], kvT[:, 1:3, 2:4, bass.ds(t * DEC_S + TP, DEC_S)]), staged, t * 8 + 6)
                one(pool.tensor_copy(kcs[:], kcT[:, :, bass.ds(t, 1), :].squeeze(2)), staged, t * 8 + 7)
                one(pool.tensor_copy(hvs[:], hv[:, :, bass.ds(t, 1), :].squeeze(2)), staged, t * 8 + 8)
            def attend(i, g2, more):
                t = i + 4 * g2
                for j in range(4):
                    if j == 3 and more:
                        pool.wait_ge(pv_mm, t + 1)
                    read_out(pool, MRG.g0, t, 4, j)
                    pool.dma_start(mgate[t * 4 + j], mg[:, j % 2]).then_inc(mg_out[j % 2], 16)
                    if j == 0 and more:
                        pool.wait_ge(scored, t * 3 + 3)
                        pool.wait_ge(s_read, t * 3 + 3)
                        load_bias(t + 1)
                        load_keys(t + 1)
                    if j == 1 and more:
                        pool.wait_ge(extra_mm, t + 1)
                        stage(t + 1)
                if more:
                    load_values(t + 1)

            load_keys(0)
            stage(0)
            load_values(0)
            pool.dma_start(out["kv"], kvT[:]).then_inc(stored, 16)
            pool.wait_ge(pool_c, 9)
            pool.wait_ge(st_conv, 8)
            pool.dma_start(out["conv"], cstash[:]).then_inc(stored, 16)
            pool.dma_start(out["h"], hstash[:]).then_inc(stored, 16)
            with pool.Fori(0, 4) as i:
                attend(i, 0, True)
            with pool.Fori(0, 3) as i:
                attend(i, 1, True)
            attend(3, 1, False)
            pool.wait_ge(mg_out[0], 16 * 16)
            pool.wait_ge(mg_out[1], 16 * 16)
            pool.wait_ge(o_ok, 16)
            src = mgate.rearrange("(k n) p t -> n p k t", k=2)
            for n in range(2):
                pool.dma_start(mgl[:, n], src[n]).then_inc(mgl_in[n], 16)
            pool.wait_ge(osp_lo, 4)
            pool.wait_ge(stored, 48)
            pool.dma_start(z[:], a["x"]).then_inc(z_in, 16)
            with pool.Fori(1, DC // 2) as i:
                for n in range(2):
                    pool.wait_ge(m_add, i * 2 + (n - 1))
                    pool.dma_start(mgl[:, n], src[i * 2 + n]).then_inc(mgl_in[n], 16)
            for q in range(8):
                pool.wait_ge(mod_f, 8 + q + 1)
                pool.wait_ge(mod_hi, 8 + q + 1)
                one(pool.tensor_tensor(xlo[:, 2 * q:2 * q + 2, :], sq[:, q % 2], f32(xhi[:, 2 * q:2 * q + 2, :]), ALU.subtract),
                    mod_lo2, q + 1)

        @block.tensor
        def _(pe):
            def g_unit(st_, i, j, kin, parts, ready=None):
                s, k = st_.rawG(i, j)
                e = (st_.g0 + j) % 2
                pe.wait_ge(raw_used[s], k + 1)
                three(e, kin, parts, ready).then_inc(unit_done, 1)

            def three(e, kin, parts, ready=None):
                for b, k0, mh, ml, c0, start, stop in parts:
                    for kk in range(kin):
                        if ready:
                            ready(k0 + kk)
                        w = slice((k0 + kk) * P, (k0 + kk + 1) * P)
                        acc = bank[b][:, 0:T]
                        pe.matmul(acc, wlo[e][:, w], mh[:, c0 + kk, :], start=start and kk == 0, stop=False)
                        pe.matmul(acc, whi[e][:, w], ml[:, c0 + kk, :], start=False, stop=False)
                        m = pe.matmul(acc, whi[e][:, w], mh[:, c0 + kk, :], start=False, stop=stop and kk == kin - 1)
                return m

            def a_units(st_, i, us):
                for u in us:
                    s, k = st_.raw(i, st_.A[u])
                    pe.wait_ge(raw_in[s], k * 16 + 16)
                    for q in range(4):
                        ins = pe.matmul(bank[6 + u // 4 % 2][32 * q:32 * q + 32, :], condp[:, 4 * q + u % 4, :],
                                        raw[:, s, q * 512:(q + 1) * 512], start=u % 4 == 0, stop=u % 4 == 3)
                    ins.then_inc(raw_used[s], 1)

            def a_turn(q):
                pe.wait_ge(ada_cp, q + 1)
                after(pe, ada_out, q)
                for e in range(4):
                    ins = pe.matmul(bank[4][:, 16 * e:16 * e + NSEQ], adp[:, e, :], selq[:], start=True, stop=True)
                ins.then_inc(ada_t, 1)

            def quad(st_, i, m):
                return i * (len(st_.A) // 4) + (st_.a0 // 4 + m)

            pe.wait_ge(cond_ok, 1)

            def init(i):
                for m in range(2):
                    a_units(INIT, i, range(4 * m, 4 * m + 4))
                    if isinstance(i, int) and m == 0:
                        pe.wait_ge(a_in, 32)
                    a_turn(quad(INIT, i, m))

            steps(pe, INIT.n, init)

            pe.wait_ge(pool_set, N_POOL)
            pe.wait_ge(dve_set, 1)
            pe.matmul(bank[5][0:H, 0:RV], rel1[:], ohr[:, 4:4 + RV], start=True, stop=True)
            for s in range(DEC_S):
                pe.matmul(bank[2][:, 0:PAST + DEC_S], selt[:, s, :], ohr[:, 3 - s:3 - s + PAST + DEC_S],
                          start=s == 0, stop=s == 3)
            for s in range(DEC_S):
                ins = pe.matmul(bank[3][:, 0:NCMP], selt[:, s, :],
                                ohr[:, 34 - s:34 - s + STRIDE * NCMP:STRIDE], start=s == 0, stop=s == 3)
            ins.then_inc(bias_mm, 1)

            X = (xhi, xlo)
            pe.wait_ge(glo_done, 1)
            three(0, DC, [(0, 0, *X, 0, True, True)], lambda kk: kk % 2 == 0 and pe.wait_ge(mod_lo, kk // 2 + 1)).then_inc(unit_done, 1)

            def plain(st_, i, j, ready=None):
                b = (st_.g0 + j) % 2
                after(pe, acc_free[b], i * (len(st_.G) // 2) + (st_.g0 + j) // 2)
                g_unit(st_, i, j, DC, [(b, 0, *X, 0, True, True)], ready)

            def a_between(st_, i, j):
                if j % 2 == 0:
                    a_units(st_, i, range(j, j + 2))
                elif j == 3:
                    a_turn(quad(st_, i, 0))

            for j in range(8):
                plain(QS, 0, j)
                if j in (3, 5):
                    a_units(QS, 0, range(j - 3, j - 1))
                elif j == 6:
                    a_turn(quad(QS, 0, 0))
            with pe.Fori(0, KVS.n) as i:
                for j in range(4):
                    plain(KVS, i, j)
                    a_between(KVS, i, j)

            read_out(pe, 0, 0, 2, 0)
            for tt in range(2):
                ins = pe.transpose(bank[5][:, tt * 48:tt * 48 + 48], gT[:, tt * P:(tt + 1) * P], ident[0:48, 0:48])
            ins.then_inc(gate_t, 1)
            kv_written(pe)
            for br in range(2):
                for tt in range(2):
                    for g2 in range(2):
                        ins = pe.transpose(bank[2 + br][:, (tt * 2 + g2) * P:(tt * 2 + g2 + 1) * P],
                                           kvT[:, 1 + br, 2 + g2, tt * P:(tt + 1) * P], ident[:])
            ins.then_inc(vt_mm, 1)

            def compress(kv):
                pe.wait_ge(w1_in[kv], 16)
                pe.wait_ge(w_in_s, 16 * 6)
                pe.wait_ge(rows_in, 16 * 17 * (kv + 1))
                pe.wait_ge(rows_cp, 2 + kv)
                pe.wait_ge(gt_ok, 1)
                after(pe, kc_ok, 2 * kv)
                for l in range(CMP):
                    for h in range(2):
                        half = slice(64 * h, 64 * h + 64)
                        ins = pe.matmul(bank[5][half, 0:(2 * NSEQ + 1) * NCMP], w1d[half, l, :],
                                        cmp_rows[half, :, l:l + STRIDE * (NCMP - 1) + 1:STRIDE], start=l == 0, stop=l == CMP - 1)
                ins.then_inc(cmp_mm, 1)

            def compress_out(kv):
                pe.wait_ge(cmp_act, kv + 1)
                if kv == 0:
                    pe.matmul(bank[5][:, 0:2 * NSEQ * NCMP], w2b[:, 0, :], hk[:], start=True, stop=True).then_inc(w2_mm, 1)
                else:
                    for g2 in range(2):
                        ins = pe.matmul(bank[5][0:NCMP, g2 * P:(g2 + 1) * P], hv[:, g2, DEC_B, :], w2b[:, 1, :],
                                        start=True, stop=True)
                    ins.then_inc(w2_mm, 1)

            def recurrent(i, kv=None):
                for j in range(4):
                    plain(RNN, i, j)
                    a_between(RNN, i, j)
                    if kv is not None and j == 0:
                        compress(kv)
                    if kv is not None and j == 1:
                        compress_out(kv)
                    if j % 2:
                        c = i * 2 + j // 2
                        pe.wait_ge(conv_ok, c + 1)
                        pe.wait_ge(wc_ok, c + 1)
                        after(pe, rg_act, c)
                        pe.wait_ge(vt_ok, 1)
                        for w in range(2):
                            ins = pe.matmul(bank[2 + w][:, 0:L], wcur[:, w, :], xc[:, 0:L], start=True, stop=True)
                        ins.then_inc(rgate_mm, 1)

            recurrent(0, 0)
            with pe.Fori(1, RNN.n - 1) as i:
                recurrent(i)
            recurrent(RNN.n - 1, 1)
            pe.wait_ge(kc_ok, 3)

            def attend(i, g2):
                t = i + 4 * g2

                def unit(j):
                    b = (MRG.g0 + j) % 2
                    pe.wait_ge(acc_free[b], t * 2 + (MRG.g0 + j) // 2)
                    g_unit(MRG, t, j, DC, [(b, 0, *X, 0, True, True)])

                if isinstance(i, int):
                    a_units(MID, 0, range(4))
                unit(0)
                if isinstance(i, int):
                    a_turn(quad(MID, 0, 0))
                    pe.wait_ge(ada_out, quad(MID, 0, 0) + 1)
                pe.wait_ge(staged, t * 8 + 8)
                for h in range(2):
                    for br in range(2):
                        pe.matmul(bank[4][:, (h * 2 + br) * P:(h * 2 + br + 1) * P], qz[:, h, 0:P],
                                  kvT[:, 1 + br, g2, 0:P], start=True, stop=True)
                for qt in range(2):
                    for h in range(2):
                        c = (qt * 2 + h) * NCMP
                        ins = pe.matmul(bank[5][:, c:c + NCMP], qz[:, h, qt * P:(qt + 1) * P], kcT[:, g2, DEC_B, :],
                                        start=True, stop=True)
                ins.then_inc(scored, 1)
                after(pe, o_ok, t * 2)
                for h in range(2):
                    for br in range(2):
                        ins = pe.matmul(bank[2 + h][:, br * TP:(br + 1) * TP], qz[:, h, P:TP],
                                        kvT[:, 1 + br, g2, 0:TP], start=True, stop=True)
                ins.then_inc(scored, 1)
                pe.wait_ge(k_in, t * 48 + 48)
                for br in range(2):
                    for g in range(KVH):
                        pe.matmul(bank[6 + br][32 * g:32 * g + 32, 0:PAST + DEC_S], qzs[:, g, :], ks[:, br, g // 2, :],
                                  start=True, stop=True)
                for g in range(KVH):
                    ins = pe.matmul(bank[6][32 * g:32 * g + 32, 264:264 + NCMP], qzs[:, g, :], kcs[:, g // 2, :],
                                    start=True, stop=True)
                ins.then_inc(scored, 1)
                unit(1)
                pe.wait_ge(s_read, t * 3 + 1)
                for br in range(2):
                    for g in range(2):
                        pe.transpose(bank[4][0:DEC_S, (br * 2 + g) * P:(br * 2 + g + 1) * P], vn[:, br, g, :], ident[:])
                for g in range(2):
                    ins = pe.matmul(bank[5][0:NCMP, g * P:(g + 1) * P], hvs[:, g, :], w2b[:, 1, :], start=True, stop=True)
                ins.then_inc(extra_mm, 1)
                unit(2)
                pe.wait_ge(p_ok, t * 3 + 1)
                pe.wait_ge(extra_ok, t + 1)
                for c in range(4):
                    pe.transpose(bank[4][:, c * P:(c + 1) * P], pb[:, 0, c * P:(c + 1) * P], ident[:])
                for c in range(4):
                    ins = pe.transpose(bank[5][0:NCMP, c * P:(c + 1) * P], pcs[:, c, :], ident[:])
                ins.then_inc(pt_mm, 1)
                pe.wait_ge(p_ok, t * 3 + 2)
                pe.wait_ge(s_read, t * 3 + 3)
                for h in range(2):
                    for c in range(4):
                        ins = pe.transpose(bank[2 + h][:, c * P:(c + 1) * P], pb[:, 1 + h, c * P:(c + 1) * P], ident[:])
                ins.then_inc(pt_mm, 1)
                pe.wait_ge(p_ok, t * 3 + 3)
                for c in range(4):
                    pe.transpose(bank[6][:, c * P:(c + 1) * P], pss[:, c // 2, (c % 2) * P:(c % 2 + 1) * P], ident[:])
                for br in range(2):
                    pe.transpose(bank[7][0:DEC_S, br * P:(br + 1) * P], pss[:, br, PAST:PAST + DEC_S], ident[:])
                pe.transpose(bank[7][0:NCMP, 2 * P:3 * P], pcc[:], ident[:]).then_inc(pt_mm, 1)
                unit(3)
                pe.wait_ge(pt_act, t * 3 + 3)
                pe.wait_ge(pt_dve, t + 1)
                pe.wait_ge(v_in, t * 48 + 48)
                for qt in range(2):
                    todo = [(br, kt) for br in range(2) for kt in range(qt + 1)]
                    for n, (br, kt) in enumerate([(None, None)] + todo):
                        for h in range(2):
                            dims = slice(g2 * P + 64 * h, g2 * P + 64 * h + 64)
                            o_ = bank[2][64 * h:64 * h + 64, qt * P:(qt + 1) * P]
                            if n == 0:
                                pe.matmul(o_, vcp[:, dims], pcT[:, (qt * 2 + h) * P:(qt * 2 + h + 1) * P], start=True, stop=False)
                                continue
                            p_ = pT[:, 0, (h * 2 + br) * P:(h * 2 + br + 1) * P] if qt == 0 else \
                                pT[:, 1 + h, (br * 2 + kt) * P:(br * 2 + kt + 1) * P]
                            v0 = kt * 256 + dims.start
                            pe.matmul(o_, vtok[:, br, v0:v0 + 64], p_, start=False, stop=n == len(todo))
                for g_ in range(2):
                    pair = [(g, bank[3][64 * (g % 2):64 * (g % 2) + 64, g_ * 16:g_ * 16 + 16], slice(64 * g, 64 * g + 64))
                            for g in (2 * g_, 2 * g_ + 1)]
                    for g, o_, dims in pair:
                        pe.matmul(o_, vcs[:, dims], psc[:, 32 * g:32 * g + 16], start=True, stop=False)
                    for br in range(2):
                        for g, o_, dims in pair:
                            pe.matmul(o_, vnew[:, br * 256 + dims.start:br * 256 + dims.stop],
                                      psn[:, br * P + 32 * g:br * P + 32 * g + 16], start=False, stop=False)
                    for c in range(4):
                        for g, o_, dims in pair:
                            ins = pe.matmul(o_, vs[:, c // 2, c % 2, dims], psT[:, c * P + 32 * g:c * P + 32 * g + 16],
                                            start=False, stop=c == 3)
                ins.then_inc(pv_mm, 1)

            steps(pe, 4, lambda i: attend(i, 0))
            with pe.Fori(0, 4) as i:
                attend(i, 1)

            pe.wait_ge(o_ok, 16)

            def merge(i):
                for j in range(4):
                    b = (CMB.g0 + j) % 2
                    pe.wait_ge(acc_free[b], i * 2 + (CMB.g0 + j) // 2)
                    ready = None
                    if isinstance(i, int) and j == 0:
                        def ready(kk):
                            if kk % 2 == 0:
                                pe.wait_ge(osp_lo, kk // 2 + 1)
                    g_unit(CMB, i, j, RC, [(b, 0, ohi, olo, 0, True, True), (2 + b, RC, yhi, ylo, 0, True, True)], ready)
                    a_between(CMB, i, j)

            steps(pe, CMB.n, merge)
            def out_(i):
                for j in range(4):
                    plain(OUT, i, j, (lambda kk: pe.wait_ge(m_ok, kk + 1)) if isinstance(i, int) and j == 0 else None)

            steps(pe, OUT.n, out_)

            def norm(n):
                if n == 0:
                    a_units(LNA, 0, range(4))
                pe.wait_ge(zs_add, DC * (n + 1))
                pe.matmul(bank[2][:, 0:T], ones[:], zsum[:], start=True, stop=True).then_inc(ln_mean, 1)
                for q in range(8):
                    pe.wait_ge(ln_sq, 8 * n + q + 1)
                    for c in range(2):
                        ins = pe.matmul(bank[3][:, 0:T], ones[:], sq[:, q % 2, c, :], start=q == 0 and c == 0,
                                        stop=q == 7 and c == 1)
                    ins.then_inc(ln_var, 1)

            norm(0)
            a_turn(quad(LNA, 0, 0))
            a_units(LNA, 0, range(4, 12))
            a_turn(quad(LNA, 0, 1))
            for half in range(2):
                st_, o0 = FIN[half], O_FIN[half]

                def fin(i):
                    for j in range(4):
                        b = (o0 + j) % 2
                        pe.wait_ge(acc_free[b], i * 2 + (o0 + j) // 2)
                        ready = None
                        if half == 0 and j == 0 and isinstance(i, int):
                            def ready(kk):
                                if kk == 10:
                                    a_turn(quad(LNA, 0, 2))
                                if kk % 2 == 0:
                                    pe.wait_ge(mod_lo2, kk // 2 + 1)
                        g_unit(FIN[half], i, j, DC, [(b, 0, *X, 0, True, True)], ready)

                steps(pe, st_.n, fin)

                def fout(i):
                    for j in range(4):
                        if isinstance(i, int) and j < 2:
                            pe.wait_ge(h_lo, HALF * half + KS * (j + 1))
                        b = (O_FOUT[half] + j // 2) % 2
                        if j % 2 == 0:
                            pe.wait_ge(acc_free[b], i + (O_FOUT[half] + j // 2) // 2)
                        g_unit(FOUT[half], i, j, KS, [(b, 0, hhi, hlo, KS * (j % 2), j % 2 == 0, j % 2 == 1)])

                steps(pe, FOUT[half].n, fout)
            norm(1)

        @block.scalar
        def _(act):
            act.dma_start(bada[:], a["b_ada"]).then_inc(a_in, 16)
            act.dma_start(selq[:], a["selq"]).then_inc(a_in, 16)
            act.wait_ge(c_in, 16)
            act.wait_ge(pool_set, 1)
            nc.scalar.activation(condp[:, :, 0:NSEQ], cond[:], ACT.Silu).then_inc(cond_ok, 1)
            act.dma_start(xt[:], a["x"]).then_inc(x_in, 16)
            small = ((lnp, "lnp"), (ident, "ident"), (ohr, "ohr"),
                     (rel1[0:32, :], "rel"), (maskC, "mask_c"), (graw, "w_gate"), (qb, "b_q"), (kvb, "b_kv"), (gb, "b_gate"),
                     (rb, "b_r"), (convw, "conv_w"), (lrup, "lru_p"), (cst, "conv_state"), (h0t, "rnn_h"),
                     (btanh, "b_merge"), (ptab, "page_table"))
            assert len(small) == N_SMALL
            for dst, name in small:
                act.dma_start(dst if isinstance(dst, bass.AP) else dst[:], a[name]).then_inc(b_in, 16)

            def a_copy(st_, i, m):
                s, k = st_.raw(i, st_.A[4 * m + 3])
                after(act, ada_t, i * (len(st_.A) // 4) + (st_.a0 // 4 + m))
                act.wait_ge(raw_used[s], k + 1)
                nc.scalar.copy(adp[:].rearrange("p e n -> p (e n)"), bank[6 + m % 2][:]).then_inc(ada_cp, 1)

            def mod_high(n, tm, q, slot):
                act.wait_ge(mod_f, q + (8 * n + 1))
                nc.scalar.copy(xhi[:, bass.ds(q * 2, 2), :], tm[:, slot]).then_inc(mod_hi, 1)

            def init(i):
                for m in range(2):
                    a_copy(INIT, i, m)
                    if not (isinstance(i, int) and m == 0):
                        mod_high(0, xm, i * 2 + (m - 1), 1 - m)

            init(0)
            act.wait_ge(b_in, SMALL)
            act.wait_ge(pool_set, N_POOL)
            nc.scalar.copy(whi[0][:].rearrange("p (k n) -> p k n", n=P)[:, :, 0:48], graw[:]).then_inc(hi_done, 1)
            act.wait_ge(dve_set, 2)
            nc.scalar.activation(sp[:, 1, :], sp[:, 0, :], ACT.Exp, scale=-1.0).then_inc(act_set, 1)
            with act.Fori(1, INIT.n) as i:
                init(i)
            mod_high(0, xm, 7, 1)
            s, k = QS.rawG(0, 0)
            act.wait_ge(raw_in[s], 16 * k + 16)
            nc.scalar.copy(whi[1][:], raw[:, s]).then_inc(hi_done, 1)
            act.wait_ge(unit_done, 1)
            nc.scalar.activation(gT[:], bank[0][0:48, 0:T], ACT.Sigmoid, bias=gb[:]).then_inc(acc_free[0], 1)
            for j in range(8):
                split_hi(act, QS, 0, j + 1)
                if j == 6:
                    a_copy(QS, 0, 0)
            with act.Fori(0, KVS.n) as i:
                for j in range(4):
                    split_hi(act, KVS, i, j + 1)
                    if j == 2:
                        a_copy(KVS, i, 0)

            def compress_act(kv):
                act.wait_ge(cmp_mm, kv + 1)
                n = 2 * NSEQ * NCMP
                nc.scalar.copy(cbias[:], bank[5][:, n:n + 1]).then_inc(cb_ok, 1)
                act.wait_ge(cb_ok, kv + 1)
                dst = hk[:] if kv == 0 else hv[:].rearrange("p g s n -> p (g s n)")
                nc.scalar.activation(dst, bank[5][:, 0:n], ACT.Silu, bias=cbias[:]).then_inc(cmp_act, 1)

            def compress_copy(kv):
                act.wait_ge(w2_mm, kv + 1)
                n = 2 * NSEQ * NCMP
                if kv == 0:
                    nc.scalar.copy(kcT[:].rearrange("p g s n -> p (g s n)"), bank[5][:, 0:n]).then_inc(kc_ok, 2)
                else:
                    nc.scalar.copy(vcp[:], bank[5][0:NCMP, 0:256]).then_inc(kc_ok, 1)

            act.wait_ge(dve_set, 3)

            def recurrent(i, kv=None):
                for j in range(4):
                    c = i * 2 + j // 2
                    if j == 0:
                        if isinstance(i, int) and i == 0:
                            split_hi(act, RNN, i, 1)
                        split_hi(act, RNN, i, 2)
                    if j == 2:
                        split_hi(act, RNN, i, 4)
                    if kv is not None and j == 0:
                        compress_act(kv)
                    if kv is not None and j == 1:
                        compress_copy(kv)
                    if j == 2:
                        a_copy(RNN, i, 0)
                    if j % 2:
                        act.wait_ge(unit_done, RNN.g(i, j) + 1)
                        after(act, y_ok, c)
                        b = (RNN.g0 + j) % 2
                        nc.scalar.activation(gy[:], bank[b][:, 0:T], ACT.Gelu_apprx_tanh,
                                             bias=rb[:, 1, bass.ds(c, 1)]).then_inc(acc_free[b], 1)
                        if j == 1 or not isinstance(i, int) or i < RNN.n - 1:
                            split_hi(act, RNN, i, j + 2)
                        act.wait_ge(rgate_mm, c + 1)
                        nc.scalar.activation(rg[:, 0:L], bank[2][:, 0:L], ACT.Tanh, bias=lrup[:, 1, bass.ds(c, 1)],
                                             scale=0.5).then_inc(act_c, 1)
                        nc.scalar.activation(ig[:, 0:L], bank[3][:, 0:L], ACT.Tanh, bias=lrup[:, 2, bass.ds(c, 1)],
                                             scale=0.5).then_inc(rg_act, 1)
                        act.wait_ge(act_c, c + 1)
                        nc.scalar.activation(th[:, 0:L], rg[:, 0:L], ACT.Tanh, scale=sp[:, 4, bass.ds(c, 1)],
                                             bias=sp[:, 4, bass.ds(c, 1)])
                        nc.scalar.activation(av[:, 0:L], rg[:, 0:L], ACT.Exp, scale=sp[:, 5, bass.ds(c, 1)],
                                             bias=sp[:, 5, bass.ds(c, 1)]).then_inc(gy_ok, 1)
                        act.wait_ge(q_ok, c + 1)
                        nc.scalar.activation(rg[:, 0:L], rg[:, 0:L], ACT.Sqrt, scale=0.25).then_inc(sq_ok, 1)

            recurrent(0, 0)
            with act.Fori(1, RNN.n - 1) as i:
                recurrent(i)
            recurrent(RNN.n - 1, 1)
            a_copy(MID, 0, 0)

            def merge_gate(t, j):
                b = (MRG.g0 + j) % 2
                act.wait_ge(unit_done, MRG.g(t, j) + 1)
                after(act, mg_out[j % 2], t * 32 + 16 * (j // 2))
                n = t * 4 + j
                nc.scalar.activation(mg[:, j % 2], bank[b][:, 0:T], ACT.Tanh, scale=0.5,
                                     bias=btanh[:, bass.ds(n, 1)]).then_inc(acc_free[b], 1)

            def attend(i, g2):
                t = i + 4 * g2

                def expo(x, col, acc=True):
                    return nc.scalar.activation(x, x, ACT.Exp, bias=st[:, 1, col:col + 1],
                                                accum_out=st[:, 2, col:col + 1])

                split_hi(act, MRG, t, 1)
                split_hi(act, MRG, t, 2)
                merge_gate(t, 0)
                act.wait_ge(s_read, t * 3 + 1)
                for c in range(4):
                    expo(pb[:, 0, c * P:(c + 1) * P], c)
                nc.scalar.activation(pcs[:], pcs[:], ACT.Exp).then_inc(exped, 1)
                act.wait_ge(s_read, t * 3 + 2)
                for c in range(4):
                    ins = expo(pb[:, 1 + c // 2, (c % 2) * TP:(c % 2 + 1) * TP], 4 + c)
                ins.then_inc(exped, 1)
                act.wait_ge(s_read, t * 3 + 3)
                expo(pss[:, 0, :], 8)
                expo(pss[:, 1, :], 9)
                expo(pcc[:], 10).then_inc(exped, 1)
                split_hi(act, MRG, t, 3)
                merge_gate(t, 1)
                act.wait_ge(extra_mm, t + 1)
                after(act, pv_mm, t)
                nc.scalar.copy(vnew[:], bank[4][0:DEC_S, :])
                nc.scalar.copy(vcs[:], bank[5][0:NCMP, 0:256]).then_inc(extra_ok, 1)
                split_hi(act, MRG, t, 4)
                merge_gate(t, 2)
                act.wait_ge(pt_mm, t * 3 + 2)
                nc.scalar.copy(pT[:, 1, :], bank[2][:])
                nc.scalar.copy(pT[:, 2, :], bank[3][:]).then_inc(pt_act, 1)
                act.wait_ge(pt_mm, t * 3 + 3)
                nc.scalar.copy(psT[:], bank[6][:]).then_inc(pt_act, 1)
                nc.scalar.copy(psn[:], bank[7][0:DEC_S, 0:2 * P])
                nc.scalar.copy(psc[:], bank[7][0:NCMP, 2 * P:3 * P]).then_inc(pt_act, 1)
                merge_gate(t, 3)

            steps(act, 4, lambda i: attend(i, 0))
            with act.Fori(0, 4) as i:
                attend(i, 1)
            act.wait_ge(o_ok, 16)
            act.wait_ge(mg_out[0], 256)
            act.wait_ge(mg_out[1], 256)
            for dst, src in ((ohi, qT), (yhi, yv)):
                for q in range(4):
                    nc.scalar.copy(dst[:, 2 * q:2 * q + 2, :], src[:, 2 * q:2 * q + 2, :]).then_inc(osp_hi, 1)
            with act.Fori(0, CMB.n) as i:
                for j in range(4):
                    n = i * 4 + j
                    split_hi(act, CMB, i, j + 1)
                    if j == 2:
                        a_copy(CMB, i, 0)
                    act.wait_ge(m_add, n + 1)
                    nc.scalar.activation(xhi[:, bass.ds(n, 1), :].squeeze(1), mt[:, 0, :], ACT.Copy, scale=0.5).then_inc(m_hi, 1)
            with act.Fori(0, OUT.n) as i:
                for j in range(4):
                    split_hi(act, OUT, i, j + 1)

            def norm_act(n):
                if n == 0:
                    a_copy(LNA, 0, 0)
                for q in range(8):
                    act.wait_ge(ln_c, 8 * n + q + 1)
                    after(act, ln_var, 8 * n + q - 1)
                    nc.scalar.activation(sq[:, q % 2], z[:, 2 * q:2 * q + 2, :], ACT.Square).then_inc(ln_sq, 1)
                act.wait_ge(ln_var, 8 * n + 8)
                nc.scalar.activation(rstd[:], bank[3][:, 0:T], ACT.Sqrt, bias=epst[:]).then_inc(ln_std, 1)
                for c in range(DC if n == 0 else DC - 4):
                    act.wait_ge(ln_n, 8 * n + c // 2 + 1)
                    nc.scalar.activation(z[:, c, :], z[:, c, :], ACT.Identity, scale=lnp[:, n, 0, c:c + 1],
                                         bias=lnp[:, n, 1, c:c + 1]).then_inc(ln_out, 1)
                    if n == 0 and c % 2 and c > 1:
                        mod_high(1, sq, c // 2 - 1, (c // 2 - 1) % 2)
                    if n == 0 and c in (5, 9):
                        a_copy(LNA, 0, c // 4)

            norm_act(0)
            mod_high(1, sq, 7, 1)
            for half in range(2):
                def fin(i, last):
                    for j in range(4):
                        split_hi(act, FIN[half], i, j + 1, KUNIT if last and j == 3 else UNIT)
                        c = i * 2 + (j // 2 + HALF * half)
                        b = (O_FIN[half] + j) % 2
                        act.wait_ge(unit_done, FIN[half].g(i, j) + 1)
                        if j % 2 == 0:
                            act.wait_ge(h_lo, c - 1) if not (isinstance(c, int) and c < 1) else None
                            nc.scalar.activation(ht[:, j // 2], bank[b][:, 0:T], ACT.Silu).then_inc(acc_free[b], 1)
                        else:
                            read_out(act, O_FIN[half], i, 4, j)
                            nc.scalar.copy(hhi[:, bass.ds(i * 2 + j // 2, 1), :].squeeze(1), ht[:, j // 2]).then_inc(h_hi, 1)

                def fout(i, last):
                    for j in range(4):
                        if last and j == 3:
                            if half == 0:
                                split_hi(act, FOUT[half], i, j + 1, UNIT)
                        else:
                            split_hi(act, FOUT[half], i, j + 1, KUNIT)

                fin(0, False)
                with act.Fori(1, FIN[half].n - 1) as i:
                    fin(i, False)
                fin(FIN[half].n - 1, True)
                with act.Fori(0, FOUT[half].n - 1) as i:
                    fout(i, False)
                fout(FOUT[half].n - 1, True)
            norm_act(1)

        @block.vector
        def _(dve):
            ch = Chain(dve, dve_c)
            v = nc.vector
            dve.wait_ge(a_in, 32)
            for n in range(2):
                scales = bada[:, 3 * DC * n:3 * DC * n + 2 * DC].rearrange("p (m k) -> p m k", k=4)[:, :, 2:4]
                gates_ = bada[:, 3 * DC * n + 2 * DC:3 * DC * (n + 1)]
                v.tensor_scalar(scales, scales, 1.0, None, ALU.add)
                ch(v.tensor_scalar(gates_, gates_, 1.0, None, ALU.add))
            def a_out(q):
                dve.wait_ge(ada_t, q + 1)
                v.tensor_tensor(ada[:, bass.ds(q * 4, 4), :], bank[4][:, 0:64].rearrange("p (e s) -> p e s", e=4)[:, :, 0:NSEQ],
                                bc(bada[:, bass.ds(q * 4, 4)], NSEQ), ALU.add).then_inc(ada_out, 1)

            def quad(st_, i, m):
                return i * (len(st_.A) // 4) + (st_.a0 // 4 + m)

            def mod_full(n, src, tm, q, slot):
                def sh(c, s0, s1):
                    return ada[:, bass.ds(q * 4 + (3 * DC * n + c), 1), s0:s1].squeeze(1)

                for c in range(2):
                    v.tensor_scalar(tm[:, slot, c, 0:TP], src[:, bass.ds(q * 2 + c, 1), 0:TP].squeeze(1), sh(2 + c, 0, 1),
                                    sh(c, 0, 1), ALU.mult, ALU.add)
                new = grp(tm[:, slot], 0, 2)
                cols_ = src[:, bass.ds(q * 2, 2), TP:T].rearrange("p c (b s) -> p c b s", s=DEC_S)
                ch(v.tensor_tensor(new, cols_, bc(ada[:, bass.ds(q * 4 + (3 * DC * n + 2), 2), 1:NSEQ], DEC_S), ALU.mult))
                v.tensor_tensor(new, new, bc(ada[:, bass.ds(q * 4 + 3 * DC * n, 2), 1:NSEQ], DEC_S), ALU.add).then_inc(mod_f, 1)

            def mod_low(n, tm, q, slot):
                dve.wait_ge(mod_hi, q + (8 * n + 1))
                v.tensor_tensor(xlo[:, bass.ds(q * 2, 2), :], tm[:, slot], f32(xhi[:, bass.ds(q * 2, 2), :]),
                                ALU.subtract).then_inc(mod_lo, 1)
                dve.wait_ge(mod_lo, q + (8 * n + 1))

            def init(i):
                ch.loop(i if isinstance(i, int) else i - 1, 2)
                for m in range(2):
                    q = quad(INIT, i, m)
                    a_out(q)
                    if isinstance(i, int) and m == 0:
                        dve.wait_ge(x_in, 16)
                    dve.wait_ge(ada_out, q + 1)
                    mod_full(0, xt, xm, q, m)
                    if not (isinstance(i, int) and m == 0):
                        mod_low(0, xm, q - 1, 1 - m)

            init(0)
            ch.end(1)
            dve.wait_ge(b_in, SMALL)
            dve.wait_ge(pool_set, N_POOL)
            for s in range(DEC_S):
                for h in range(2):
                    ins = v.tensor_copy(selt[:, s, :].rearrange("k (g m) -> k g m", m=32)[:, h:KVH:2, s:16:DEC_S],
                                        rel1[:].rearrange("k (g r h) -> k g r h", g=2, h=2)[:, :, :, h])
            ins.then_inc(dve_set, 1)
            v.tensor_scalar(btanh[:], btanh[:], 0.5, None, ALU.mult)
            lam = lrup[:, 3, :]
            ch(v.tensor_scalar(sp[:, 1, :], lam, -1.0, None, ALU.mult))
            v.tensor_tensor(sp[:, 0, :], lam, sp[:, 1, :], ALU.max).then_inc(dve_set, 1)
            dve.wait_ge(act_set, 1)
            e_, z_, z2, s_ = sp[:, 1, :], sp[:, 2, :], sp[:, 3, :], sp[:, 4, :]
            ch(v.tensor_scalar(z_, e_, 2.0, None, ALU.add))
            ch(v.reciprocal(z_, z_))
            ch(v.tensor_tensor(z_, z_, e_, ALU.mult))
            ch(v.tensor_tensor(z2, z_, z_, ALU.mult))
            ch(v.tensor_scalar(s_, z2, 1.0 / 15, None, ALU.mult))
            for n in (13, 11, 9, 7, 5, 3):
                ch(v.scalar_tensor_tensor(s_, s_, 1.0 / n, z2, ALU.add, ALU.mult))
            ch(v.scalar_tensor_tensor(s_, s_, 1.0, z_, ALU.add, ALU.mult))
            ch(v.tensor_scalar(e_, lam, -1.0, 0.0, ALU.mult, ALU.max))
            ch(v.scalar_tensor_tensor(s_, s_, 2.0, e_, ALU.mult, ALU.add))
            ch(v.tensor_scalar(sp[:, 5, :], s_, -0.5 * LRU_C, None, ALU.mult))
            ch(v.tensor_scalar(lrup[:, 1:3, :], lrup[:, 1:3, :], 0.5, None, ALU.mult))
            v.tensor_scalar(s_, s_, 0.5 * LRU_C, None, ALU.mult).then_inc(dve_set, 1)
            dve.wait_ge(hi_done, 1)
            v.tensor_tensor(wlo[0][:].rearrange("p (k n) -> p k n", n=P)[:, :, 0:48], graw[:],
                            f32(whi[0][:].rearrange("p (k n) -> p k n", n=P)[:, :, 0:48]), ALU.subtract).then_inc(glo_done, 1)
            with dve.Fori(1, INIT.n) as i:
                init(i)
            ch.end(INIT.n - 1)
            mod_low(0, xm, 7, 1)
            dve.wait_ge(bias_mm, 1)
            v.tensor_copy(rrow[:], bank[5][0:H, 0:RV])
            v.tensor_copy(biasS[:], bank[2][:, 0:PAST + DEC_S])
            v.tensor_copy(biasCS[:], bank[3][:, 0:NCMP]).then_inc(bias_ok, 1)

            dve.wait_ge(hi_done, 2)
            s, _k = QS.rawG(0, 0)
            v.tensor_tensor(wlo[1][:], raw[:, s], f32(whi[1][:]), ALU.subtract).then_inc(raw_used[s], 1)
            for j in range(8):
                b = (QS.g0 + j) % 2
                split_lo(dve, QS, 0, j + 1)
                if j == 7:
                    a_out(quad(QS, 0, 0))
                dve.wait_ge(unit_done, QS.g(0, j) + 1)
                v.tensor_scalar(qT[:, j, :], bank[b][:, 0:T], qb[:, j:j + 1], SCALE, ALU.add, ALU.mult).then_inc(acc_free[b], 1)
            with dve.Fori(0, KVS.n) as i:
                for j in range(4):
                    b = (KVS.g0 + j) % 2
                    split_lo(dve, KVS, i, j + 1)
                    if j == 3:
                        a_out(quad(KVS, i, 0))
                    dve.wait_ge(unit_done, KVS.g(i, j) + 1)
                    v.tensor_scalar(kvT[:, bass.ds(i, 1), j, :].squeeze(1), bank[b][:, 0:T], kvb[:, bass.ds(i, 1), j],
                                    None, ALU.add).then_inc(acc_free[b], 1)
            dve.wait_ge(gate_t, 1)
            v.tensor_copy(gtok[:].rearrange("p t n -> p (t n)"), bank[5][:, 0:96]).then_inc(gt_ok, 1)
            dve.wait_ge(vt_mm, 1)
            v.tensor_copy(vtok[:, 0, :], bank[2][:])
            v.tensor_copy(vtok[:, 1, :], bank[3][:]).then_inc(vt_ok, 1)

            def chain_rnn(c):
                dve.wait_ge(gy_ok, c + 1)
                ch(v.tensor_tensor(rg[:, 0:L], av[:, 0:L], av[:, 0:L], ALU.mult))
                v.scalar_tensor_tensor(rg[:, 0:L], rg[:, 0:L], 1.0, th[:, 0:L], ALU.add, ALU.mult).then_inc(q_ok, 1)
                v.tensor_tensor(ah[:], starts(av, 1)[:, :, 0], h0t[:, bass.ds(c, 1), :].squeeze(1), ALU.mult)
                ch(v.scalar_tensor_tensor(ig[:, 0:L], ig[:, 0:L], 1.0, xc[:, 0:L], ALU.add, ALU.mult))
                v.memset(starts(av, 1), 0.0)
                dve.wait_ge(sq_ok, c + 1)
                ch(v.tensor_tensor(rg[:, 0:L], rg[:, 0:L], ig[:, 0:L], ALU.mult))
                ch(v.tensor_tensor(starts(rg, 1)[:, :, 0], starts(rg, 1)[:, :, 0], ah[:], ALU.add))
                ch(v.tensor_tensor_scan(th[:, 0:L], av[:, 0:L], rg[:, 0:L], 0.0, ALU.mult, ALU.add))
                v.tensor_copy(hstash[:, bass.ds(c, 1), 0:1].squeeze(1), th[:, TP - 1:TP])
                v.tensor_copy(hstash[:, bass.ds(c, 1), 1:NSEQ].squeeze(1), starts(th, 4)[:, :, 3])
                v.tensor_tensor(yv[:, bass.ds(c, 1), 0:TP].squeeze(1), th[:, 0:TP], gy[:, 0:TP], ALU.mult)
                v.tensor_tensor(yv[:, bass.ds(c, 1), TP:T].squeeze(1).rearrange("p (b s) -> p b s", s=DEC_S), starts(th, 4),
                                gy[:, TP:T].rearrange("p (b s) -> p b s", s=DEC_S), ALU.mult).then_inc(y_ok, 1)

            def recurrent(i, before=True):
                for j in range(4):
                    c = i * 2 + j // 2
                    split_lo(dve, RNN, i, j + 1)
                    if j == 0 and before:
                        chain_rnn(i * 2 - 1)
                    if j == 2:
                        chain_rnn(i * 2)
                    if j % 2 == 0:
                        b = (RNN.g0 + j) % 2
                        dve.wait_ge(unit_done, RNN.g(i, j) + 1)
                        bias = rb[:, 0, bass.ds(c, 1)]
                        after(dve, st_conv, c)
                        v.tensor_scalar(rxp[:, 3:3 + TP], bank[b][:, 0:TP], bias, None, ALU.add)
                        v.tensor_scalar(starts(rxp, 7, TP + 3)[:, :, 3:7],
                                        bank[b][:, TP:T].rearrange("p (b s) -> p b s", s=DEC_S), bias, None,
                                        ALU.add).then_inc(acc_free[b], 1)
                        read_out(dve, RNN.g0, i, 4, j)
                        dve.wait_ge(st_pre, c + 2)
                        w = [convw[:, k, bass.ds(c, 1)] for k in range(4)]
                        ch(v.tensor_scalar(xc[:, 0:L], rxp[:, 3:3 + L], w[3], lrup[:, 0, bass.ds(c, 1)], ALU.mult, ALU.add))
                        for k in range(3):
                            ins = v.scalar_tensor_tensor(xc[:, 0:L], rxp[:, k:k + L], w[k], xc[:, 0:L], ALU.mult, ALU.add)
                            if k < 2:
                                ch(ins)
                        ins.then_inc(conv_ok, 1)
                    if j == 3:
                        a_out(quad(RNN, i, 0))
            recurrent(0, False)
            with dve.Fori(1, RNN.n) as i:
                ch.loop(i - 1, 16)
                recurrent(i)
            ch.end(RNN.n - 1)
            chain_rnn(2 * RNN.n - 1)

            NEGMAX = -3.0e38
            a_out(quad(MID, 0, 0))
            for g2 in range(2):
                with dve.Fori(0, 4) as i:
                    t = i + 4 * g2
                    ch.loop(i, 15)
                    split_lo(dve, MRG, t, 1)
                    dve.wait_ge(scored, t * 3 + 1)
                    dve.wait_ge(bz_in, t * 32 + 32)

                    def scores(out_, ps, bias, col):
                        return v.tensor_tensor_reduce(out_, ps, bias, 1.0, NEGMAX, ALU.add, ALU.max, st[:, 0, col:col + 1])

                    c5 = bank[5][:, 0:4 * NCMP].rearrange("p (q h n) -> p q h n", q=2, h=2)
                    pc4 = pcs[:].rearrange("p (q h) n -> p q h n", q=2)
                    for q in range(2):
                        x0 = CMP - 1 + P * (1 - q)
                        v.tensor_tensor(pc4[:, q], c5[:, q], bz[:, :, x0:x0 + STRIDE * (NCMP - 1) + 1:STRIDE], ALU.add)
                    for c in range(4):
                        ins = scores(pb[:, 0, c * P:(c + 1) * P], bank[4][:, c * P:(c + 1) * P], bz[:, c // 2, P:TP], c)
                    ch(ins)
                    ch(v.tensor_reduce(stc[:, 0, :], pcs[:], AX.X, ALU.max))
                    v.tensor_scalar(st[:, 1, 0:4], st[:, 0, 0:4], -1.0, None, ALU.mult)
                    v.tensor_tensor(pcs[:], pcs[:], bc(stc[:, 0, :], NCMP), ALU.subtract).then_inc(s_read, 1)
                    dve.wait_ge(scored, t * 3 + 2)
                    split_lo(dve, MRG, t, 2)
                    for c in range(4):
                        ins = scores(pb[:, 1 + c // 2, (c % 2) * TP:(c % 2 + 1) * TP],
                                     bank[2 + c // 2][:, (c % 2) * TP:(c % 2 + 1) * TP], bz[:, c // 2, 0:TP], 4 + c)
                    m1 = ch.mark(ins)
                    dve.wait_ge(scored, t * 3 + 3)
                    ch.wait(m1)
                    v.tensor_scalar(st[:, 1, 4:8], st[:, 0, 4:8], -1.0, None, ALU.mult).then_inc(s_read, 1)
                    for br in range(2):
                        scores(pss[:, br, :], bank[6 + br][:, 0:PAST + DEC_S], biasS[:], 8 + br)
                    ch(scores(pcc[:], bank[6][:, 264:264 + NCMP], biasCS[:], 10))
                    v.tensor_scalar(st[:, 1, 8:11], st[:, 0, 8:11], -1.0, None, ALU.mult).then_inc(s_read, 1)

                    gt = gtok[:, :, bass.ds(t * 6, 6)].rearrange("p q (h b) -> p q h b", b=3)
                    dve.wait_ge(exped, t * 3 + 1)
                    ch(v.reciprocal(st[:, 3, 0:4], st[:, 2, 0:4]))
                    ch(v.tensor_tensor(pc4, pc4, maskC[:].unsqueeze(2).broadcast_to([P, 2, 2, NCMP]), ALU.mult))
                    ch(v.tensor_tensor(st[:, 3, 0:4].rearrange("p (h b) -> p h b", b=2),
                                       st[:, 3, 0:4].rearrange("p (h b) -> p h b", b=2), gt[:, 0, :, 1:3], ALU.mult))
                    p0_ = pb[:, 0, :].rearrange("p (c n) -> p c n", n=P)
                    v.tensor_tensor(p0_, p0_, bc(st[:, 3, 0:4], P), ALU.mult)
                    ch(v.tensor_reduce(stc[:, 1, :], pcs[:], AX.X, ALU.add))
                    ch(v.tensor_scalar(stc[:, 1, :], stc[:, 1, :], 1e-30, None, ALU.max))
                    ch(v.reciprocal(stc[:, 2, :], stc[:, 1, :]))
                    c2 = stc[:, 2, :].rearrange("p (q h) -> p q h", q=2)
                    ch(v.tensor_tensor(c2, c2, gt[:, :, :, 0], ALU.mult))
                    v.tensor_tensor(pcs[:], pcs[:], bc(stc[:, 2, :], NCMP), ALU.mult).then_inc(p_ok, 1)
                    split_lo(dve, MRG, t, 3)
                    dve.wait_ge(exped, t * 3 + 2)
                    ch(v.reciprocal(st[:, 3, 4:8], st[:, 2, 4:8]))
                    w1_ = st[:, 3, 4:8].rearrange("p (h b) -> p h b", b=2)
                    ch(v.tensor_tensor(w1_, w1_, gt[:, 1, :, 1:3], ALU.mult))
                    p1_ = pb[:, 1:3, :].rearrange("p h (b n) -> p (h b) n", n=TP)
                    v.tensor_tensor(p1_, p1_, bc(st[:, 3, 4:8], TP), ALU.mult).then_inc(p_ok, 1)
                    dve.wait_ge(exped, t * 3 + 3)
                    ch(v.reciprocal(st[:, 3, 8:11], st[:, 2, 8:11]))
                    gst = gs[:, bass.ds(t, 1), :].squeeze(1)
                    v.tensor_tensor(st[:, 3, 8:10], st[:, 3, 8:10], gst[:, 1:3], ALU.mult)
                    ch(v.tensor_tensor(st[:, 3, 10:11], st[:, 3, 10:11], gst[:, 0:1], ALU.mult))
                    v.tensor_tensor(pss[:], pss[:], bc(st[:, 3, 8:10], PAST + DEC_S), ALU.mult)
                    v.tensor_scalar(pcc[:], pcc[:], st[:, 3, 10:11], None, ALU.mult).then_inc(p_ok, 1)
                    split_lo(dve, MRG, t, 4)
                    dve.wait_ge(pt_mm, t * 3 + 1)
                    v.tensor_copy(pT[:, 0, :], bank[4][:])
                    v.tensor_copy(pcT[:], bank[5][0:NCMP, :]).then_inc(pt_dve, 1)
                    dve.wait_ge(pv_mm, t + 1)
                    dve.wait_ge(staged, t * 8 + 8)
                    v.tensor_copy(qT[:, bass.ds(t, 1), 0:TP].squeeze(1), bank[2][:, 0:TP]).then_inc(o_ok, 1)
                    v.tensor_copy(qT[:, :, bass.ds(t * DEC_S + TP, DEC_S)],
                                  bank[3][:, 0:32].rearrange("p (c s) -> p c s", s=DEC_S)).then_inc(o_ok, 1)
                ch.end(4)

            for n, (dst, src, hi) in enumerate(((olo, qT, ohi), (ylo, yv, yhi))):
                for q in range(4):
                    dve.wait_ge(osp_hi, 4 * n + q + 1)
                    v.tensor_tensor(dst[:, 2 * q:2 * q + 2, :], src[:, 2 * q:2 * q + 2, :], f32(hi[:, 2 * q:2 * q + 2, :]),
                                    ALU.subtract).then_inc(osp_lo, 1)
            with dve.Fori(0, CMB.n) as i:
                for j in range(4):
                    n = i * 4 + j
                    b = (CMB.g0 + j) % 2
                    split_lo(dve, CMB, i, j + 1)
                    if j == 3:
                        a_out(quad(CMB, i, 0))
                    dve.wait_ge(unit_done, CMB.g(i, j) + 1)
                    dve.wait_ge(mgl_in[j % 2], i * 32 + 16 * (j // 2 + 1))
                    v.scalar_tensor_tensor(mt[:, 0, :], mgl[:, j % 2, 0, :], 1.0, bank[b][:, 0:T], ALU.add, ALU.mult)
                    v.scalar_tensor_tensor(mt[:, 1, :], mgl[:, j % 2, 1, :], 1.0, bank[2 + b][:, 0:T], ALU.add,
                                           ALU.mult).then_inc(acc_free[b], 1)
                    read_out(dve, CMB.g0, i, 4, j)
                    v.tensor_tensor(mt[:, 0, :], mt[:, 0, :], mt[:, 1, :], ALU.add).then_inc(m_add, 1)
                    dve.wait_ge(m_hi, n + 1)
                    v.scalar_tensor_tensor(xlo[:, bass.ds(n, 1), :].squeeze(1), mt[:, 0, :], 0.5,
                                           f32(xhi[:, bass.ds(n, 1), :].squeeze(1)), ALU.mult, ALU.subtract).then_inc(m_ok, 1)
                    dve.wait_ge(m_ok, n + 1)

            def gated(o0, i, per, j, g, keep, z0, final):
                b, n = (o0 + j) % 2, i * per + j
                v.tensor_scalar(zt[:, 0:TP], bank[b][:, 0:TP], ada[:, bass.ds(n + g, 1), 0:1].squeeze(1), None, ALU.mult)
                v.tensor_tensor(zt[:, TP:T].rearrange("p (b s) -> p b s", s=DEC_S),
                                bank[b][:, TP:T].rearrange("p (b s) -> p b s", s=DEC_S),
                                bc(ada[:, bass.ds(n + g, 1), 1:NSEQ].squeeze(1), DEC_S), ALU.mult).then_inc(acc_free[b], 1)
                read_out(dve, o0, i, per, j)
                zc = z[:, bass.ds(n, 1), :].squeeze(1)
                v.scalar_tensor_tensor(zc, zc, keep, zt[:], ALU.mult, ALU.add).then_inc(z_ok, 1)
                dve.wait_ge(z_ok, n + (z0 + 1))
                if final:
                    v.tensor_tensor(zsum[:], zsum[:], zc, ALU.add).then_inc(zs_add, 1)
                    dve.wait_ge(zs_add, n + (DC * (final - 1) + 1))

            dve.wait_ge(z_in, 16)
            ch(v.memset(zsum[:], 0.0))
            with dve.Fori(0, OUT.n) as i:
                for j in range(4):
                    split_lo(dve, OUT, i, j + 1)
                    dve.wait_ge(unit_done, OUT.g(i, j) + 1)
                    gated(OUT.g0, i, 4, j, 2 * DC, ALPHA, 0, 1)

            def norm_dve(n):
                dve.wait_ge(ln_mean, n + 1)
                ch(v.tensor_copy(mean[:], bank[2][:, 0:T]))

                def over(q):
                    return z[:, 2 * q:2 * q + 2, :]

                for q in range(8):
                    v.tensor_tensor(over(q), over(q), mean[:].unsqueeze(1).broadcast_to([P, 2, T]),
                                    ALU.subtract).then_inc(ln_c, 1)
                if n == 0:
                    a_out(quad(LNA, 0, 0))
                dve.wait_ge(ln_std, n + 1)
                ch(v.reciprocal(rstd[:], rstd[:]))

                def scaled(q):
                    v.tensor_tensor(over(q), over(q), rstd[:].unsqueeze(1).broadcast_to([P, 2, T]),
                                    ALU.mult).then_inc(ln_n, 1)

                scaled(0)
                for q in range(8):
                    if q < 7:
                        scaled(q + 1)
                    if n == 0:
                        dve.wait_ge(ln_out, 2 * q + 2)
                        after(dve, mod_lo2, q - 1)
                        mod_full(1, z, sq, q, q % 2)
                        if q == 5:
                            a_out(quad(LNA, 0, 1))
                if n == 0:
                    a_out(quad(LNA, 0, 2))
                else:
                    dve.wait_ge(ln_n, 16)
                    for c in range(DC - 4, DC):
                        v.tensor_scalar(z[:, c, :], z[:, c, :], lnp[:, n, 0, c:c + 1], lnp[:, n, 1, c:c + 1], ALU.mult,
                                        ALU.add).then_inc(ln_last, 1)

            norm_dve(0)
            ch(v.memset(zsum[:], 0.0))
            for half in range(2):
                def fin(i, last):
                    for j in range(4):
                        split_lo(dve, FIN[half], i, j + 1, KUNIT if last and j == 3 else UNIT)
                        if j % 2:
                            c = i * 2 + (j // 2 + HALF * half)
                            b = (O_FIN[half] + j) % 2
                            dve.wait_ge(unit_done, FIN[half].g(i, j) + 1)
                            read_out(dve, O_FIN[half], i, 4, j - 1)
                            v.tensor_tensor(ht[:, j // 2], ht[:, j // 2], bank[b][:, 0:T], ALU.mult).then_inc(acc_free[b], 1)
                            read_out(dve, O_FIN[half], i, 4, j)
                            dve.wait_ge(h_hi, c + 1)
                            hc = bass.ds(i * 2 + j // 2, 1)
                            v.tensor_tensor(hlo[:, hc, :].squeeze(1), ht[:, j // 2], f32(hhi[:, hc, :].squeeze(1)),
                                            ALU.subtract).then_inc(h_lo, 1)

                def fout(i, last):
                    for j in range(4):
                        if last and j == 3:
                            if half == 0:
                                split_lo(dve, FOUT[half], i, j + 1, UNIT)
                        else:
                            split_lo(dve, FOUT[half], i, j + 1, KUNIT)
                        if j % 2:
                            dve.wait_ge(unit_done, FOUT[half].g(i, j) + 1)
                            gated(O_FOUT[half], i, 2, j // 2, 5 * DC, ALPHA if half == 0 else 1.0, DC * (1 + half),
                                  2 * half)

                with dve.Fori(0, FIN[half].n - 1) as i:
                    fin(i, False)
                fin(FIN[half].n - 1, True)
                with dve.Fori(0, FOUT[half].n - 1) as i:
                    fout(i, False)
                fout(FOUT[half].n - 1, True)
            norm_dve(1)


def lay_out(x_prompt, x_sample, c_prompt, c_sample, cache_cmp_kv, cache_slc_kv, cache_win_kv, state_conv, state_rnn_h,
            page_table, rel_bias, w_ada, b_ada, w_in, b_in, cmp_pos, cmp_w1, cmp_w2, w_attn_o, conv_w, conv_b, lru_wa,
            lru_ba, lru_wi, lru_bi, lru_lambda, w_rnn_o, w_out, w_ffn_in, w_ffn_out, ln_g, ln_b):
    import numpy as np

    heads = np.array([[j % 4 + 8 * (j // 4), j % 4 + 8 * (j // 4) + 4] for j in range(NP_)])
    hcols = (heads.reshape(-1)[:, None] * HD + np.arange(HD)).reshape(-1)

    def blocks(w, kc=None):
        k, n = w.shape
        return w.reshape(k // P, P, n // P, P).transpose(2, 1, 0, 3).reshape(n // P, P, -1)

    def cols(v_):
        return np.ascontiguousarray(v_.reshape(-1, P).T)

    w, b = w_in[0], b_in[0]
    cuts = np.cumsum([H * HD, 512, 512, 512, 3 * H, DR, DR, 2 * D])
    wq, wkv, wg = w[:, :cuts[0]], w[:, cuts[0]:cuts[3]], w[:, cuts[3]:cuts[4]]
    wrx, wry, wm = w[:, cuts[4]:cuts[5]], w[:, cuts[5]:cuts[6]], w[:, cuts[6]:]
    gcols = (heads.reshape(-1)[:, None] * 3 + np.arange(3)).reshape(-1)
    pairs = np.arange(DC).reshape(-1, 2)
    ada_order = np.concatenate([np.concatenate([np.concatenate([m + 3 * DC * n, m + 3 * DC * n + DC]) for m in pairs]
                                               + [np.arange(DC) + 3 * DC * n + 2 * DC]) for n in range(2)])
    wa = w_ada[0].reshape(4, 4, P, NADA, P)[:, :, :, ada_order].reshape(4, 4, P, NADA // 4, 4 * P)
    wa = wa.transpose(3, 1, 2, 0, 4).reshape(NADA, P, UNIT)
    wr = np.stack([blocks(wrx), blocks(wry)], 1).reshape(2 * RC, P, -1)
    ao, ro = blocks(w_attn_o[0][hcols]), blocks(w_rnn_o[0])
    comb = np.concatenate([ao, ro], 2)
    wo = blocks(w_out[0])
    fi = w_ffn_in[0]
    ff = np.stack([blocks(fi[:, :FF]), blocks(fi[:, FF:])], 1).reshape(2 * FC, P, -1)

    def woven(st_, g, a_):
        out_, gi, ai = [], 0, st_.a0
        for _ in range(st_.n):
            for p in range(st_.U):
                if p in st_.G:
                    out_.append(g[gi])
                    gi += 1
                else:
                    out_.append(a_[ai])
                    ai += 1
        return out_

    def led(st_, g):
        return [g[0]] + list(wa[st_.a0:st_.a_end]) + list(g[1:])

    units = np.stack(woven(INIT, [], wa) + woven(QS, blocks(wq[:, hcols]), wa) + woven(KVS, blocks(wkv), wa)
                     + woven(RNN, wr, wa) + led(MID, blocks(wm)) + woven(CMB, comb, wa) + list(wo) + led(LNA, ff))
    fo = w_ffn_out[0].reshape(2, 2, KS, P, DC, P).transpose(0, 4, 1, 3, 2, 5).reshape(4 * DC, P, KUNIT)

    x = np.concatenate([x_prompt.reshape(TP, D), x_sample.reshape(TS, D)], 0)
    c = np.concatenate([c_prompt, c_sample], 0)

    def feat(m):
        return np.ascontiguousarray(m.reshape(m.shape[0], -1, P).transpose(2, 1, 0))

    def keys(k_):
        n, t = k_.shape[:2]
        return np.ascontiguousarray(k_.reshape(n, t, 2, 2, HD).transpose(0, 3, 4, 2, 1).reshape(n, P, 2, t))

    slc, cmp_, win = cache_slc_kv[0], cache_cmp_kv[0], cache_win_kv[0]
    n_phys = slc.shape[0]

    dist = np.arange(0, 512)
    exact = 16
    ratio = np.log(np.maximum(dist, 1).astype(np.float32) / np.float32(exact)) / np.float32(np.log(128 / exact))
    bucket = np.where(dist < exact, dist, np.minimum(exact + (ratio * np.float32(32 - exact)).astype(np.int32), 31))

    def one_hot(dists):
        m = np.zeros((33, len(dists)), np.float32)
        for n, d in enumerate(dists):
            if d >= 0:
                m[bucket[d], n] = 1.0
            else:
                m[32, n] = NEG
        return m

    mask = np.zeros((P, 2, NCMP), np.float32)
    for qt in range(2):
        for n in range(NCMP):
            mask[:, qt, n] = (np.arange(P) + qt * P - (STRIDE * n + CMP - 1)) >= 0
    selq = np.zeros((P, NSEQ), np.float32)
    for q in range(4):
        selq[32 * q + np.arange(NSEQ), np.arange(NSEQ)] = 1.0
    pos = cmp_pos[0].transpose(0, 2, 1)
    w1 = cmp_w1[0].transpose(0, 2, 1, 3)
    ins = {
        "w_units": units, "w_ffn_out_units": fo, "x": feat(x), "cond": feat(c),
        "b_ada": cols(b_ada[0])[:, ada_order], "lnp": np.stack([np.stack([cols(ln_g[0][n]), cols(ln_b[0][n])], 1) for n in range(2)], 1),
        "ident": np.eye(P, dtype=np.float32), "selq": selq, 
        "ohr": one_hot(259 - np.arange(4 + RV)), "rel": rel_bias[:, heads.reshape(-1)], "mask_c": mask,
        "w_gate": wg[:, gcols].reshape(DC, P, 48).transpose(1, 0, 2), "b_q": cols(b[:cuts[0]][hcols]),
        "b_kv": cols(b[cuts[0]:cuts[3]]).reshape(P, 3, 4), "b_gate": b[cuts[3]:cuts[4]][gcols].reshape(48, 1),
        "b_r": cols(b[cuts[4]:cuts[6]]).reshape(P, 2, RC), "conv_w": np.stack([cols(conv_w[0][k]) for k in range(4)], 1),
        "lru_p": np.stack([cols(m[0]) for m in (conv_b, lru_ba, lru_bi, lru_lambda)], 1),
        "conv_state": state_conv[0].reshape(DEC_B, 3, RC, P).transpose(3, 2, 0, 1), "rnn_h": feat(state_rnn_h[0]),
        "b_merge": cols(b[cuts[6]:]), "page_table": page_table.reshape(1, -1),
        "cmp_w1": np.concatenate([w1, w1], 1), "cmp_w2": cmp_w2[0], "cmp_pos": np.concatenate([pos, pos], 1),
        "lru_wa": lru_wa[0], "lru_wi": lru_wi[0],
        "cmp_k": keys(cmp_[:, :, 0]), "cmp_v": keys(cmp_[:, :, 1]), "slc_k": keys(slc[:, :, 0]),
        "slc_v": slc[:, :, 1].reshape(n_phys, PAGE, 256), "win_k": keys(win[:, :, 0]),
        "win_v": win[:, :, 1].reshape(DEC_B, 2, P, 256).transpose(0, 2, 1, 3),
    }
    return {k_: np.ascontiguousarray(v_) for k_, v_ in ins.items()}, n_phys


_OUTS = {"y": [P, DC, T], "kv": [P, 3, 4, T], "conv": [P, RC, NSEQ, 3], "h": [P, RC, NSEQ]}


def kernel(**inputs):
    import numpy as np
    import concourse.bacc as bacc
    from concourse.bass_utils import run_bass_kernel_spmd

    ins, n_phys = lay_out(**{k: np.asarray(v) for k, v in inputs.items()})
    nc = bacc.Bacc("TRN2", target_bir_lowering=False, num_devices=1)
    arrays = {f"in_{k}": v for k, v in ins.items()}
    a = {k: nc.dram_tensor(f"in_{k}", list(v.shape), mybir.dt.from_np(v.dtype), kind="ExternalInput").ap()
         for k, v in ins.items()}
    a["n_phys"] = n_phys
    out = {k: nc.dram_tensor(f"out_{k}", s, F32, kind="ExternalOutput").ap() for k, s in _OUTS.items()}
    build(nc, a, out)
    r = run_bass_kernel_spmd(nc, [arrays], core_ids=[0]).results[0]
    y = r["out_y"].transpose(2, 1, 0).reshape(T, D)
    kv = r["out_kv"].reshape(2, HD, 3, 2, 2, T).transpose(2, 5, 3, 4, 0, 1).reshape(3, T, 2, KVH, HD)
    conv = r["out_conv"].transpose(2, 3, 1, 0).reshape(NSEQ, 3, DR)
    h = r["out_h"].transpose(2, 1, 0).reshape(NSEQ, DR)
    c_ = np.ascontiguousarray
    kvp = [c_(kv[k, :TP])[None, None] for k in range(3)]
    kvs = [c_(kv[k, TP:].reshape(DEC_B, DEC_S, 2, KVH, HD))[None] for k in range(3)]
    return (c_(y[:TP])[None], c_(y[TP:]).reshape(DEC_B, DEC_S, D), kvp[0], kvp[1], kvp[2], c_(conv[:1])[None], c_(h[:1])[None],
            kvs[0], kvs[1], kvs[2], c_(conv[1:])[None], c_(h[1:])[None])
```
